# Optimizing a Trainium2 kernel written in Bass

```python
import jax, jax.numpy as jnp
from jax import lax
import numpy as np
import math

D_MODEL = 1024
BATCH = 1
SEQ = 256
DEPTH = 1

D_MIX = D_MODEL
SC_WIDTH = D_MIX // 4
SC_GROUPS = 4
SC_KERNEL = 3
GDN_WIDTH = D_MIX // 2
GDN_HEADS = 4
GDN_HEAD_DIM = GDN_WIDTH // GDN_HEADS
GDN_CONV = 4
GDN_CHUNK = 64
SB_WIDTH = D_MIX - SC_WIDTH - GDN_WIDTH
SB_HEADS = 4
SB_HEAD_DIM = SB_WIDTH // SB_HEADS
SB_BLOCK = 128
D_FF = 256 * ((8 * D_MODEL // 3 + 255) // 256)
FFN_CONV = 3
NORM_EPS = 1e-6
SPLIT_SIZES = (SC_WIDTH, SC_WIDTH, SC_WIDTH,
               GDN_WIDTH, GDN_WIDTH, GDN_WIDTH, GDN_WIDTH, GDN_HEADS, GDN_HEADS,
               SB_WIDTH, SB_WIDTH, SB_WIDTH)
D_IN_PROJ = 3 * SC_WIDTH + 4 * GDN_WIDTH + 2 * GDN_HEADS + 3 * SB_WIDTH


def rmsnorm(x, w):
    xf = x.astype(jnp.float32)
    y = xf * lax.rsqrt(jnp.mean(xf * xf, axis=-1, keepdims=True) + NORM_EPS) * w.astype(jnp.float32)
    return y.astype(x.dtype)

def l2norm(x):
    xf = x.astype(jnp.float32)
    return xf * lax.rsqrt(jnp.sum(xf * xf, axis=-1, keepdims=True) + NORM_EPS)

def causal_dwconv(x, w):
    K, C = w.shape
    return lax.conv_general_dilated(
        x, w[:, None, :].astype(x.dtype), window_strides=(1,), padding=[(K - 1, 0)],
        dimension_numbers=('NWC', 'WIO', 'NWC'), feature_group_count=C)

def split_columns(proj):
    points = [int(p) for p in np.cumsum(np.array(SPLIT_SIZES))[:-1]]
    return jnp.split(proj, points, axis=-1)

def gated_delta_rule_chunked(q, k, v, g, beta):
    f32 = jnp.float32
    Bsz, L, H, Dk = q.shape
    Dv = v.shape[-1]
    N = L // GDN_CHUNK

    def to_chunks(t):
        t = t.reshape((Bsz, N, GDN_CHUNK, H) + t.shape[3:])
        return jnp.moveaxis(t, 3, 1)

    q = to_chunks(q.astype(f32)) * (Dk ** -0.5)
    k = to_chunks(k.astype(f32))
    v = to_chunks(v.astype(f32))
    beta = to_chunks(beta.astype(f32))
    g = jnp.cumsum(to_chunks(g.astype(f32)), axis=-1)
    idx = jnp.arange(GDN_CHUNK)
    causal = idx[:, None] >= idx[None, :]
    strict = idx[:, None] > idx[None, :]
    decay = jnp.exp(jnp.where(causal, g[..., :, None] - g[..., None, :], -jnp.inf))
    k_beta = k * beta[..., None]
    lower = jnp.where(strict, jnp.einsum('bhncd,bhnsd->bhncs', k_beta, k) * decay, 0.0)
    lhs = lower + jnp.eye(GDN_CHUNK, dtype=f32)
    rhs = jnp.concatenate([v * beta[..., None], k_beta * jnp.exp(g)[..., None]], axis=-1)
    sol = lax.linalg.triangular_solve(lhs, rhs, left_side=True, lower=True, unit_diagonal=True)
    u, w = sol[..., :Dv], sol[..., Dv:]
    attn_intra = jnp.where(causal, jnp.einsum('bhncd,bhnsd->bhncs', q, k) * decay, 0.0)

    def step(S, inp):
        q_i, k_i, u_i, w_i, g_i, a_i = inp
        v_new = u_i - jnp.einsum('bhcd,bhde->bhce', w_i, S)
        o = jnp.einsum('bhcd,bhde->bhce', q_i * jnp.exp(g_i)[..., None], S) + \
            jnp.einsum('bhcs,bhse->bhce', a_i, v_new)
        g_last = g_i[..., -1]
        S = S * jnp.exp(g_last)[..., None, None] + \
            jnp.einsum('bhcd,bhce->bhde', k_i * jnp.exp(g_last[..., None] - g_i)[..., None], v_new)
        return S, o

    xs = tuple(jnp.moveaxis(t, 2, 0) for t in (q, k, u, w, g, attn_intra))
    S0 = jnp.zeros((Bsz, H, Dk, Dv), f32)
    _, outs = lax.scan(step, S0, xs)
    return outs.transpose(1, 0, 3, 2, 4).reshape(Bsz, L, H, Dv)

def stick_breaking_attention(q, k, v):
    L, D = q.shape[1], q.shape[-1]
    scale = D ** -0.5
    q_off = jnp.arange(SB_BLOCK)
    outs = []
    for blk in range(L // SB_BLOCK):
        start, end = blk * SB_BLOCK, (blk + 1) * SB_BLOCK
        z = jnp.einsum('bqhd,bkhd->bhqk', q[:, start:end], k[:, :end]).astype(jnp.float32) * scale
        strict = jnp.arange(end)[None, :] < (start + q_off)[:, None]
        log_beta = jax.nn.log_sigmoid(z)
        log_one_minus = jnp.where(strict, jax.nn.log_sigmoid(-z), 0.0)
        tail = lax.cumsum(log_one_minus, axis=3, reverse=True) - log_one_minus
        A = jnp.where(strict, jnp.exp(log_beta + tail), 0.0)
        outs.append(jnp.einsum('bhqk,bkhd->bqhd', A.astype(v.dtype), v[:, :end]))
    return jnp.concatenate(outs, axis=1)

def first_inputs(seed: int = 0) -> dict:
    key = jax.random.key(seed)
    ks = jax.random.split(key, 16)
    f32 = jnp.float32
    nrm = lambda k, shape: jax.random.normal(k, shape, f32)
    dt = jnp.exp(jax.random.uniform(ks[6], (DEPTH, GDN_HEADS), f32, np.log(1e-3), np.log(1e-1)))
    return {
        'x': nrm(ks[0], (BATCH, SEQ, D_MODEL)),
        'w_norm_mix': 1.0 + 0.02 * nrm(ks[1], (DEPTH, D_MODEL)),
        'w_mix_in': nrm(ks[2], (DEPTH, D_MODEL, D_IN_PROJ)) * D_MODEL ** -0.5,
        'w_sconv': nrm(ks[3], (DEPTH, SC_KERNEL, SC_WIDTH)) * SC_KERNEL ** -0.5,
        'w_gdn_conv': nrm(ks[4], (DEPTH, GDN_CONV, 3 * GDN_WIDTH)) * GDN_CONV ** -0.5,
        'gdn_a_log': jnp.log(jax.random.uniform(ks[5], (DEPTH, GDN_HEADS), f32, 1.0, 16.0)),
        'gdn_dt_bias': dt + jnp.log(-jnp.expm1(-dt)),
        'w_gdn_norm': 1.0 + 0.02 * nrm(ks[7], (DEPTH, GDN_HEAD_DIM)),
        'w_mix_out': nrm(ks[8], (DEPTH, D_MIX, D_MODEL)) * D_MIX ** -0.5,
        'w_norm_ffn': 1.0 + 0.02 * nrm(ks[9], (DEPTH, D_MODEL)),
        'w_ffn_up': nrm(ks[10], (DEPTH, D_MODEL, 2 * D_FF)) * D_MODEL ** -0.5,
        'w_ffn_conv': nrm(ks[11], (DEPTH, FFN_CONV, 2 * D_FF)) * FFN_CONV ** -0.5,
        'w_ffn_down': nrm(ks[12], (DEPTH, D_FF, D_MODEL)) * D_FF ** -0.5,
        'w_norm_final': 1.0 + 0.02 * nrm(ks[13], (D_MODEL,)),
    }

def first_block(x, w_norm_mix, w_mix_in, w_sconv, w_gdn_conv, gdn_a_log, gdn_dt_bias, w_gdn_norm,
              w_mix_out, w_norm_ffn, w_ffn_up, w_ffn_conv, w_ffn_down, w_norm_final):
    Bsz, L, _ = x.shape
    f32 = jnp.float32
    for l in range(DEPTH):
        h = rmsnorm(x, w_norm_mix[l])
        proj = h @ w_mix_in[l]
        (sc_b, sc_c, sc_h, gq, gk, gv, gz, ga, gb, sq, sk, sv) = split_columns(proj)

        y_sc = sc_b * causal_dwconv(sc_c * sc_h, w_sconv[l])

        qkv = jax.nn.silu(causal_dwconv(jnp.concatenate([gq, gk, gv], axis=-1), w_gdn_conv[l]))
        gq, gk, gv = jnp.split(qkv, 3, axis=-1)
        heads = lambda t: t.reshape(Bsz, L, GDN_HEADS, GDN_HEAD_DIM)
        beta = jax.nn.sigmoid(gb.astype(f32))
        g = -jnp.exp(gdn_a_log[l].astype(f32)) * jax.nn.softplus(ga.astype(f32) + gdn_dt_bias[l].astype(f32))
        o = gated_delta_rule_chunked(l2norm(heads(gq)), l2norm(heads(gk)), heads(gv), g, beta)
        o = rmsnorm(o, w_gdn_norm[l]) * jax.nn.silu(heads(gz).astype(f32))
        y_gdn = o.reshape(Bsz, L, GDN_WIDTH).astype(x.dtype)

        sb_heads = lambda t: t.reshape(Bsz, L, SB_HEADS, SB_HEAD_DIM)
        y_sb = stick_breaking_attention(sb_heads(sq), sb_heads(sk), sb_heads(sv)).reshape(Bsz, L, SB_WIDTH)

        x = x + jnp.concatenate([y_sc, y_gdn, y_sb], axis=-1) @ w_mix_out[l]

        h = rmsnorm(x, w_norm_ffn[l])
        u = causal_dwconv(h @ w_ffn_up[l], w_ffn_conv[l])
        gate, val = jnp.split(u, 2, axis=-1)
        x = x + (jax.nn.silu(gate) * val) @ w_ffn_down[l]
    return rmsnorm(x, w_norm_final)


HEAD_DIM = 64
N_DIFF_HEADS = D_MODEL // 256
DIFF_WIDTH = N_DIFF_HEADS * 2 * HEAD_DIM
N_NAT_HEADS = D_MODEL // 128
NAT_WIDTH = N_NAT_HEADS * HEAD_DIM
MIX_WIDTH = DIFF_WIDTH + NAT_WIDTH
GRID_W = 64
NAT_KH_MAX = 8
NAT_KW = 16
Q_BLOCK = 128
N_EXPERTS = 32
TOP_K = 4
D_FF_EXPERT = D_MODEL
SWIGLU_LIMIT = 7.0
SWIGLU_ALPHA = 1.702
MOE_BLOCK = 128
RMS_EPS = 1e-6


def rms_norm(x, g):
    xf = x.astype(jnp.float32)
    y = xf * lax.rsqrt(jnp.mean(xf * xf, axis=-1, keepdims=True) + RMS_EPS)
    return (y * g.astype(jnp.float32)).astype(x.dtype)

def alibi_slopes(n_heads):
    i = jnp.arange(1, n_heads + 1, dtype=jnp.float32)
    return jnp.exp2(-8.0 * i / n_heads)

def diff_attention(q, k, v, lam, lam_init, g_sub):
    B, L, H, _, Dh = q.shape
    nb = L // Q_BLOCK
    slopes = alibi_slopes(H)
    kpos = jnp.arange(L, dtype=jnp.float32)
    scale = Dh ** -0.5
    qb = q.reshape(B, nb, Q_BLOCK, H, 2, Dh).transpose(1, 0, 2, 3, 4, 5)

    def block(args):
        q_blk, i = args
        s = jnp.einsum('bqhmd,bkhmd->bhmqk', q_blk, k).astype(jnp.float32) * scale
        qpos = (i * Q_BLOCK + jnp.arange(Q_BLOCK)).astype(jnp.float32)
        dist = jnp.abs(qpos[:, None] - kpos[None, :])
        s = s - slopes[None, :, None, None, None] * dist[None, None, None]
        p = jax.nn.softmax(s, axis=-1)
        a = p[:, :, 0] - lam * p[:, :, 1]
        return jnp.einsum('bhqk,bkhe->bqhe', a.astype(v.dtype), v)

    o = lax.map(block, (qb, jnp.arange(nb)))
    o = o.transpose(1, 0, 2, 3, 4).reshape(B, L, H, 2 * Dh)
    o = rms_norm(o, g_sub) * (1.0 - lam_init)
    return o.reshape(B, L, H * 2 * Dh)

def neighbourhood_attention(q, k, v, rpb):
    B, L, H, Dh = q.shape
    rows = L // GRID_W
    kh = min(NAT_KH_MAX, rows)
    scale = Dh ** -0.5
    qg = q.reshape(B, rows, GRID_W, H, Dh)
    kg = k.reshape(B, rows, GRID_W, H, Dh)
    vg = v.reshape(B, rows, GRID_W, H, Dh)
    r = jnp.arange(rows)
    row_start = jnp.clip(r - kh // 2, 0, rows - kh)
    row_idx = row_start[:, None] + jnp.arange(kh)[None, :]
    k_rows = kg[:, row_idx]
    v_rows = vg[:, row_idx]
    c = jnp.arange(GRID_W)
    col_start = jnp.clip(c - NAT_KW // 2, 0, GRID_W - NAT_KW)
    col_in = (c[None, :] >= col_start[:, None]) & (c[None, :] < col_start[:, None] + NAT_KW)
    dr = row_idx - r[:, None] + (NAT_KH_MAX - 1)
    dc = jnp.clip(c[None, :] - c[:, None], -(NAT_KW - 1), NAT_KW - 1) + (NAT_KW - 1)
    bias = rpb.astype(jnp.float32)[:, dr[:, None, :, None], dc[None, :, None, :]]
    s = jnp.einsum('brqhd,brkwhd->bhrqkw', qg, k_rows).astype(jnp.float32) * scale + bias[None]
    s = jnp.where(col_in[:, None, :], s, -jnp.inf)
    p = jax.nn.softmax(s.reshape(B, H, rows, GRID_W, kh * GRID_W), axis=-1)
    p = p.reshape(B, H, rows, GRID_W, kh, GRID_W).astype(v.dtype)
    o = jnp.einsum('bhrqkw,brkwhd->brqhd', p, v_rows)
    return o.reshape(B, L, H * Dh)

def swiglu_clamped(hh):
    x_glu = jnp.minimum(hh[..., ::2], SWIGLU_LIMIT)
    x_lin = jnp.clip(hh[..., 1::2], -SWIGLU_LIMIT, SWIGLU_LIMIT)
    return x_glu * jax.nn.sigmoid(SWIGLU_ALPHA * x_glu) * (x_lin + 1.0)

def moe_ffn(h, w_router, b_router, w1, b1, w2, b2):
    B, L, D = h.shape
    T = B * L
    hf = h.reshape(T, D)
    logits = (hf @ w_router + b_router).astype(jnp.float32)
    top_val, top_idx = lax.top_k(logits, TOP_K)
    gates = jax.nn.softmax(top_val, axis=-1)
    n_assign = T * TOP_K
    flat_e = top_idx.reshape(-1).astype(jnp.int32)
    flat_tok = jnp.arange(n_assign, dtype=jnp.int32) // TOP_K
    order = jnp.argsort(flat_e, stable=True)
    sorted_e = flat_e[order]
    counts = jnp.bincount(flat_e, length=N_EXPERTS).astype(jnp.int32)
    padded = (counts + MOE_BLOCK - 1) // MOE_BLOCK * MOE_BLOCK
    pad_end = jnp.cumsum(padded)
    pad_start = pad_end - padded
    grp_start = jnp.cumsum(counts) - counts
    rank = jnp.arange(n_assign, dtype=jnp.int32) - grp_start[sorted_e]
    dest_sorted = (pad_start[sorted_e] + rank).astype(jnp.int32)
    cap = (n_assign + N_EXPERTS * (MOE_BLOCK - 1) + MOE_BLOCK - 1) // MOE_BLOCK * MOE_BLOCK
    n_blocks = cap // MOE_BLOCK
    tok_buf = jnp.zeros((cap,), jnp.int32).at[dest_sorted].set(flat_tok[order])
    blk_start = jnp.arange(n_blocks, dtype=jnp.int32) * MOE_BLOCK
    blk_expert = jnp.minimum(jnp.searchsorted(pad_end, blk_start, side='right'), N_EXPERTS - 1)
    x_buf = hf[tok_buf].reshape(n_blocks, MOE_BLOCK, D)

    def expert_block(args):
        xb, e = args
        hh = xb @ w1[e] + b1[e]
        return swiglu_clamped(hh) @ w2[e] + b2[e]

    y_buf = lax.map(expert_block, (x_buf, blk_expert)).reshape(cap, D)
    dest = jnp.zeros((n_assign,), jnp.int32).at[order].set(dest_sorted)
    y = y_buf[dest].reshape(T, TOP_K, D)
    out = jnp.einsum('tk,tkd->td', gates.astype(y.dtype), y)
    return out.reshape(B, L, D)

def second_inputs(seed: int = 0) -> dict:
    key = jax.random.key(seed)
    ks = jax.random.split(key, 24)
    f32 = jnp.float32
    D, F = D_MODEL, D_FF_EXPERT
    n = lambda k, shape, s: jax.random.normal(k, shape, f32) * s
    return {
        "x": n(ks[0], (BATCH, SEQ, D), 1.0),
        "c": n(ks[1], (BATCH, D), 1.0),
        "w_ada": n(ks[2], (DEPTH, D, 6 * D), 0.5 * D ** -0.5),
        "b_ada": n(ks[3], (DEPTH, 6 * D), 0.02),
        "g_pre_mix": 1.0 + n(ks[4], (DEPTH, D), 0.02),
        "g_post_mix": 1.0 + n(ks[5], (DEPTH, D), 0.02),
        "w_in": n(ks[6], (DEPTH, D, 3 * MIX_WIDTH), D ** -0.5),
        "w_out": n(ks[7], (DEPTH, MIX_WIDTH, D), MIX_WIDTH ** -0.5),
        "lam_q1": n(ks[8], (DEPTH, HEAD_DIM), 0.1),
        "lam_k1": n(ks[9], (DEPTH, HEAD_DIM), 0.1),
        "lam_q2": n(ks[10], (DEPTH, HEAD_DIM), 0.1),
        "lam_k2": n(ks[11], (DEPTH, HEAD_DIM), 0.1),
        "g_subln": 1.0 + n(ks[12], (DEPTH, 2 * HEAD_DIM), 0.02),
        "nat_rpb": n(ks[13], (DEPTH, N_NAT_HEADS, 2 * NAT_KH_MAX - 1, 2 * NAT_KW - 1), 0.02),
        "g_pre_ffn": 1.0 + n(ks[14], (DEPTH, D), 0.02),
        "g_post_ffn": 1.0 + n(ks[15], (DEPTH, D), 0.02),
        "w_router": n(ks[16], (DEPTH, D, N_EXPERTS), D ** -0.5),
        "b_router": n(ks[17], (DEPTH, N_EXPERTS), 0.01),
        "w1": n(ks[18], (DEPTH, N_EXPERTS, D, 2 * F), D ** -0.5),
        "b1": n(ks[19], (DEPTH, N_EXPERTS, 2 * F), 0.01),
        "w2": n(ks[20], (DEPTH, N_EXPERTS, F, D), F ** -0.5),
        "b2": n(ks[21], (DEPTH, N_EXPERTS, D), 0.01),
    }

def second_block(x, c, w_ada, b_ada, g_pre_mix, g_post_mix, w_in, w_out,
              lam_q1, lam_k1, lam_q2, lam_k2, g_subln, nat_rpb,
              g_pre_ffn, g_post_ffn, w_router, b_router, w1, b1, w2, b2):
    B, L, D = x.shape
    splits = [DIFF_WIDTH, 2 * DIFF_WIDTH, 3 * DIFF_WIDTH,
              3 * DIFF_WIDTH + NAT_WIDTH, 3 * DIFF_WIDTH + 2 * NAT_WIDTH]
    for l in range(DEPTH):
        lam_init = 0.8 - 0.6 * math.exp(-0.3 * l)
        mod = jax.nn.silu(c) @ w_ada[l] + b_ada[l]
        sh1, sc1, gt1, sh2, sc2, gt2 = jnp.split(mod[:, None, :], 6, axis=-1)

        h = rms_norm(x, g_pre_mix[l]) * (1.0 + sc1) + sh1
        proj = h @ w_in[l]
        dq, dk, dv, nq, nk, nv = jnp.split(proj, splits, axis=-1)
        dq = dq.reshape(B, L, N_DIFF_HEADS, 2, HEAD_DIM)
        dk = dk.reshape(B, L, N_DIFF_HEADS, 2, HEAD_DIM)
        dv = dv.reshape(B, L, N_DIFF_HEADS, 2 * HEAD_DIM)
        lam = (jnp.exp(jnp.sum(lam_q1[l].astype(jnp.float32) * lam_k1[l].astype(jnp.float32)))
               - jnp.exp(jnp.sum(lam_q2[l].astype(jnp.float32) * lam_k2[l].astype(jnp.float32)))
               + lam_init)
        o_diff = diff_attention(dq, dk, dv, lam, lam_init, g_subln[l])
        o_nat = neighbourhood_attention(nq.reshape(B, L, N_NAT_HEADS, HEAD_DIM),
                                        nk.reshape(B, L, N_NAT_HEADS, HEAD_DIM),
                                        nv.reshape(B, L, N_NAT_HEADS, HEAD_DIM),
                                        nat_rpb[l])
        mix = jnp.concatenate([o_diff, o_nat], axis=-1) @ w_out[l]
        x = x + gt1 * rms_norm(mix, g_post_mix[l])

        h2 = rms_norm(x, g_pre_ffn[l]) * (1.0 + sc2) + sh2
        f = moe_ffn(h2, w_router[l], b_router[l], w1[l], b1[l], w2[l], b2[l])
        x = x + gt2 * rms_norm(f, g_post_ffn[l])
    return x


def setup_inputs(seed=0):
    out = dict(first_inputs(seed))
    for name, value in second_inputs(seed + 1).items():
        if name != "x":
            out[name + "_2"] = value
    return out


def reference(
    x, w_norm_mix, w_mix_in, w_sconv, w_gdn_conv, gdn_a_log, gdn_dt_bias, w_gdn_norm, w_mix_out,
    w_norm_ffn, w_ffn_up, w_ffn_conv, w_ffn_down, w_norm_final, c_2, w_ada_2, b_ada_2,
    g_pre_mix_2, g_post_mix_2, w_in_2, w_out_2, lam_q1_2, lam_k1_2, lam_q2_2, lam_k2_2,
    g_subln_2, nat_rpb_2, g_pre_ffn_2, g_post_ffn_2, w_router_2, b_router_2, w1_2, b1_2, w2_2,
    b2_2,
):
    x = first_block(
        x, w_norm_mix, w_mix_in, w_sconv, w_gdn_conv, gdn_a_log, gdn_dt_bias, w_gdn_norm,
        w_mix_out, w_norm_ffn, w_ffn_up, w_ffn_conv, w_ffn_down, w_norm_final,
    )
    return second_block(
        x, c_2, w_ada_2, b_ada_2, g_pre_mix_2, g_post_mix_2, w_in_2, w_out_2, lam_q1_2,
        lam_k1_2, lam_q2_2, lam_k2_2, g_subln_2, nat_rpb_2, g_pre_ffn_2, g_post_ffn_2,
        w_router_2, b_router_2, w1_2, b1_2, w2_2, b2_2,
    )


_drawn_inputs = setup_inputs


def setup_inputs(seed=0):
    import zlib

    import numpy as np

    out = dict(_drawn_inputs(seed))
    spreads = {}
    factors = {'g_post_mix_2': 2.681,
     'lam_k2_2': 8.0,
     'g_subln_2': 2.942,
     'nat_rpb_2': 5.052,
     'g_post_ffn_2': 8.0,
     'b1_2': 8.0,
     'b2_2': 8.0}
    for name, (base, spread) in spreads.items():
        noise = np.random.default_rng([zlib.crc32(name.encode()), seed]).standard_normal(out[name].shape)
        drawn = base * np.exp(spread * noise) if base else spread * noise
        out[name] = __import__('jax').numpy.asarray(drawn.astype(out[name].dtype))
    for name, factor in factors.items():
        out[name] = (out[name] * factor).astype(out[name].dtype)
    return out
```

```python
from contextlib import ExitStack

import numpy as np
import concourse.bass as bass
from concourse import mybir

F32 = mybir.dt.float32
I32 = mybir.dt.int32
ALU = mybir.AluOpType
ACT = mybir.ActivationFunctionType
AX_X = mybir.AxisListType.X

P = 128
D = 1024
L = 256
KC = D // P
T = L // P
DFF = 2816
NH = 4
M8 = T * NH
GCH = 64
NCH = L // GCH
NE = 32
TOPK = 4
CAP = 32
EPS = 1e-6
BIG = 1.0e30
NPIECE = 4096
PIN, PADA, PMO, PUP, PDN, PIN2, POUT = 7, 12, 2, 11, 6, 6, 2
FIRST = dict(inp=0)
FIRST["ada"] = FIRST["inp"] + PIN
FIRST["mo"] = FIRST["ada"] + PADA
FIRST["up"] = FIRST["mo"] + PMO
FIRST["dn"] = FIRST["up"] + PUP
FIRST["in2"] = FIRST["dn"] + PDN
FIRST["out"] = FIRST["in2"] + PIN2
NSTREAM = FIRST["out"] + POUT
NSLOT1, NSLOT = 4, 8
NPMAX = 64

CO, _at = {}, 0
for _n, _w in (("ident", P), ("ones", P), ("before", P), ("slot", P), ("row", 64), ("count", NPMAX),
               ("upto", P), ("same", P), ("after", P), ("level", 6 * P), ("dist", 2 * L),
               ("window", 64)):
    CO[_n] = (_at, _w)
    _at += _w
NCONST = _at
VO, _at = {}, 0
for _n, _w in (("norm_mix", 8), ("norm_ffn", 8), ("pre_mix", 8), ("pre_ffn", 8), ("sconv", 6),
               ("gconv", 48), ("gnorm", 1), ("subln", 1), ("lam", 4), ("c", 8), ("ab", 64),
               ("alog", 4), ("dtb", 4), ("brt", NE), ("fconv", PUP * 12), ("router", KC * NE)):
    VO[_n] = (_at, _w)
    _at += _w
NVEC = _at


def first_block_and_moe(nc, consts, vecs, stream, bada, rows, natb, w1, w2, b1, b2, x, out):
    ctx = ExitStack()
    with ctx:
        TOTAL = 53100
        mem = ctx.enter_context(nc.sbuf_tensor("mem", [P, TOTAL], F32))
        flat = ctx.enter_context(nc.psum_tensor("acc", [P, 8 * 512], F32))

        sems = {}

        def S(name):
            if name not in sems:
                sems[name] = ctx.enter_context(nc.semaphore(name))
            return sems[name]

        NORMS = [1, 2, "f", 3, "m", 4, "e"]
        SQUARES = dict(zip(NORMS, np.cumsum([T, T, T, T, 2 * T, T, 2 * T]).tolist()))

        STEPS = dict(
            pe_step=("ab_done gcol_done gb_done bb_done kk_done at_done krow vrow u w osum modc lams dsum lg pos cum pmt pp"),
            act_step=("eg dt wt_in osq orstd elam dsq do y_nat drstd ee"),
            dve_step=("sc_prod a8 screp egl_d gdt atm y_sc orinv y_gdn lamp nlam drinv y_diff mask lgs cnr cum_in"))
        STEPS = {engine: names.split() for engine, names in STEPS.items()}
        signalled = {engine: [] for engine in STEPS}

        def engine_of(name):
            return [engine for engine, names in STEPS.items() if name in names][0]

        def step(name):
            engine = engine_of(name)
            return S(engine), STEPS[engine].index(name) + 1

        def signal(name):
            engine = engine_of(name)
            signalled[engine].append(name)
            assert signalled[engine] == STEPS[engine][:len(signalled[engine])], name
            return S(engine), 1

        def at(off, n):
            return mem[:, off:off + n]

        def bank(b, n=1):
            return flat[:, 512 * b:512 * (b + n)]

        def three(ap, a):
            return ap.rearrange("p (a b) -> p a b", a=a)

        ring = three(at(0, NSLOT * NPIECE), NSLOT)
        WORK = NSLOT1 * NPIECE
        base = NSLOT * NPIECE
        X = three(at(base, 2048), T)
        XN = three(at(base + 2048, 2048), T)
        HT = three(at(base + 4096, 2048), KC)
        YT = three(at(base + 6144, 2048), KC)
        CST, VEC = base + 8192, base + 8192 + NCONST
        BC = VEC + NVEC
        EX = BC + 3072
        assert TOTAL - EX >= 5632 + 150
        WFIN, G1B, G2B = (at(BC + 1024 * i, 1024) for i in range(3))

        def const(name):
            o, w = CO[name]
            return at(CST + o, w)

        def vec(name):
            o, w = VO[name]
            return at(VEC + o, w)

        ident, ones, before, after = const("ident"), const("ones"), const("before"), const("after")
        upto, same = const("upto"), const("same")
        level = three(const("level"), 6)

        def W(i, n=1024):
            return at(WORK + 1024 * i, n)

        def E(i, n=1024, o=0):
            return at(EX + 1024 * i + o, n)

        SM = EX + 5632
        tiny = [SM]

        def small(n):
            r = at(tiny[0], n)
            tiny[0] += n
            assert tiny[0] <= TOTAL
            return r

        ssq, mean, rstd = small(4), small(2), small(2)
        A8, BET, GCOL, GLAST, EGC, EGL, BEG = (small(8) for _ in range(7))
        u8, v8, e8 = small(8), small(8), small(8)
        ea4 = small(4)
        MODC = small(32)
        GW1, GW2 = small(8), small(8)
        lam2, nlam = small(4), small(1)
        nmx, sme, rcs = small(4), small(4), small(4)
        silc = small(8)

        KT, QT, VT, GZ, ABC, BBC, EG, DT, MLT, ATM, XI, XIT, KB, KD, VB, WT = (W(i) for i in range(16))
        YL, CL, OT, U, VN = ABC, BBC, DT, XI, E(0)
        SBQ, SBK, SBV, SCP, SCB, SCY = (E(1 + i // 2, 512, 512 * (i % 2)) for i in range(6))
        SQR = E(4)
        OS = E(4)
        ST = E(5, 512)
        SB1 = at(base + 4096, 768)
        SB2 = at(base + 4096 + 768, 768)
        MODR = at(base + 2048, 1536)
        SCREP = at(base + 4096 + 1536, 256)
        GT = W(0, 22 * L)
        UC = W(6)
        UC2 = W(7)
        DQ, DK, NQ, NK, DV, NV = (W(i) for i in range(6))
        NB = W(6, 4096)
        SC = [W(10, 512), at(WORK + 10240 + 512, 512)]
        PA = [W(11, 512), at(WORK + 11 * 1024 + 512, 512)]
        PT = [W(12, 512), at(WORK + 12 * 1024 + 512, 512)]
        DO = W(13)
        DSQ = W(14)
        DRS = W(15)

        B1 = at(BC, 2048)
        B2 = at(base + 6144, 1024)
        tmp = [base + 6144 + 1024, base + 6144 + 2048]

        def temp(n):
            tmp[0] += n
            assert tmp[0] <= tmp[1]
            return at(tmp[0] - n, n)

        LG, MASK, EE, GATE, PM = (three(temp(64), T) for _ in range(5))
        LX, MR = three(temp(80), T), three(temp(80), T)
        V8, IR = three(temp(16), T), three(temp(16), T)
        GSUM, CNR, CCE, CCI, CT1 = temp(2), temp(1), temp(1), temp(1), temp(1)
        OH, RM = temp(NPMAX), temp(NPMAX)
        PP, GP = three(temp(T * NPMAX), T), three(temp(T * NPMAX), T)
        tmp = [EX, EX + 5632]
        GLU, LIN, SIG, HID, AT = (temp(256) for _ in range(5))
        YS, GS, XG = temp(256), temp(256), three(temp(256), 2)
        SEL, SG, SGT = three(temp(T * CAP), T), three(temp(256), T), temp(256)
        OHB = temp(CAP)
        PMT, GTT = temp(256), temp(256)
        passes = ctx.enter_context(nc.sbuf_tensor("passes", [1, 72], I32))
        H2R = XN
        slot_base = [len([n for n in range(NSTREAM) if n % NSLOT1 == s]) if s < NSLOT1 else 0 for s in range(NSLOT)]
        ESTEP = 4
        EPIECES = 6 * ESTEP
        assert EPIECES % NSLOT == 0

        block = ctx.enter_context(nc.Block())

        def taken(n, slots=NSLOT1):
            return n // slots + 1

        UPEEL = 3
        assert (FIRST["up"] + UPEEL) % NSLOT1 == 0 and (PUP - UPEEL) % NSLOT1 == 0

        def piece(eng, n):
            eng.wait_ge(S(f"slot{n % NSLOT1}_loaded"), 16 * taken(n))
            return ring[:, n % NSLOT1, :]

        def used(n):
            for part, one, ends in (("out", "out_k", "out_done"), ("in2", "proj2", None), ("dn", "down_k", "down_done"),
                                    ("up", "up", None), ("mo", "mo_k", "mo_done"), ("ada", "ada", None), ("inp", "proj", None)):
                if n >= FIRST[part]:
                    j = n - FIRST[part]
                    if part in ("inp", "in2"):
                        return S(one), 2 * j + 2
                    if part == "ada":
                        return S(one), j // 4 + 1
                    if part == "up":
                        return S(one), j + 1
                    last = {"mo": PMO, "dn": PDN, "out": POUT}[part] - 1
                    return (S(ends), 4) if j == last else (S(one), j + 1)

        @block.sync
        def _(sp):
            sp.dma_start(at(base, 2048), x).then_inc(S("x_in"), 16)
            sp.dma_start(at(CST, NCONST), consts).then_inc(S("const_in"), 16)
            sp.dma_start(at(VEC, NVEC), vecs).then_inc(S("vec_in"), 16)

            def load(n):
                if n >= NSLOT1:
                    sp.wait_ge(*used(n - NSLOT1))
                sp.dma_start(ring[:, n % NSLOT1, :], stream[n]).then_inc(S(f"slot{n % NSLOT1}_loaded"), 16)

            for n in range(FIRST["ada"]):
                load(n)
            sp.dma_start(at(BC, 3072), rows).then_inc(S("rows_in"), 16)
            sp.wait_ge(S("xT"), 4)
            sp.dma_start(MODR, bada).then_inc(S("bada_in"), 16)
            for n in range(FIRST["ada"], FIRST["in2"] + 4):
                load(n)
            sp.wait_ge(S("down_done"), 4)
            sp.dma_start(NB, natb).then_inc(S("natb_in"), 16)
            for n in range(FIRST["in2"] + 4, NSTREAM):
                load(n)

            def expert_piece(i, n):
                e, r = divmod(n, 6)
                src = w1[bass.ds(4 * ESTEP * i + 4 * e + r, 1)] if r < 4 else w2[bass.ds(2 * ESTEP * i + 2 * e + r - 4, 1)]
                sp.dma_start(ring[:, n % NSLOT, :], src.rearrange("a p n -> (a p) n"))\
                  .then_inc(S(f"slot{n % NSLOT}_loaded"), 16)

            for n in [s for s in range(NSLOT1) if (s - NSTREAM) % NSLOT1 < NSLOT1 - POUT] + \
                    list(range(NSLOT1, NSLOT)) + [s for s in range(NSLOT1) if (s - NSTREAM) % NSLOT1 >= NSLOT1 - POUT]:
                if n < NSLOT1:
                    sp.wait_ge(*used(NSTREAM - NSLOT1 + (n - NSTREAM) % NSLOT1))
                elif n == NSLOT1:
                    sp.wait_ge(*step("y_diff"))
                    sp.wait_ge(*step("y_nat"))
                expert_piece(0, n)
            sp.wait_ge(S("x4"), T)
            sp.dma_start(B1[0:NE, :], b1).then_inc(S("b_in"), 16)
            sp.dma_start(B2[0:NE, :], b2).then_inc(S("b_in"), 16)
            with sp.Fori(0, NE // ESTEP - 1) as i:
                for j in range(EPIECES):
                    sp.wait_ge(S("wused"), EPIECES * i + j + 1)
                    expert_piece(i, NSLOT + j)
            for n in range(NSLOT + (NE // ESTEP - 1) * EPIECES, NE * 6):
                sp.wait_ge(S("wused"), n - NSLOT + 1)
                expert_piece(0, n)
            for t in range(T):
                sp.wait_ge(S("x5"), t + 1)
                sp.dma_start(out[:, 1024 * t:1024 * t + 1024], X[:, t, :]).then_inc(S("stored"), 16)
            sp.wait_ge(S("stored"), 32)

        def pe_norm(i):
            pe = nc.tensor
            pe.wait_ge(S("xn"), T * i)
            if i == 1:
                pe.wait_ge(S("const_in"), 16)
            for k in range(KC):
                for t in range(T):
                    o = 512 * (k // 2) + 256 * (k % 2) + 128 * t
                    last = nc.tensor.transpose(flat[:, o:o + 128], XN[:, t, 128 * k:128 * k + 128], ident)
                if k % 2:
                    last.then_inc(S("xT"), 1)

        def hT_ready(pe, i):
            pe.wait_ge(S("hT_dve"), 2 * i)
            pe.wait_ge(S("hT_act"), 2 * i)

        def pe_rows(n0, nk, lhs, done, first_bank=0):
            for k in range(nk):
                wp = piece(nc.tensor, n0 + k // 4)
                for t in range(T):
                    for h in range(2):
                        last = nc.tensor.matmul(bank(first_bank + 2 * t + h), lhs[:, k, 128 * t:128 * t + 128],
                                                wp[:, 1024 * (k % 4) + 512 * h:1024 * (k % 4) + 512 * h + 512],
                                                start=(k == 0), stop=(k == nk - 1))
                        if k == nk - 1:
                            last.then_inc(S(done), 1)
                if k % 4 == 3 and k < nk - 1:
                    last.then_inc(S(done.replace("done", "k")), 1)

        def conv_free(eng, g):
            if g < 6:
                eng.wait_ge(S("gconv_done"), g + 1)
            elif g < 9:
                eng.wait_ge(S("proj_act"), g - 5)
            elif g == 9:
                eng.wait_ge(*step("sc_prod"))
            else:
                eng.wait_ge(S("proj_act"), g - 6)

        @block.tensor
        def _(pe):
            mm = nc.tensor.matmul
            pe_norm(1)
            hT_ready(pe, 1)
            pe.wait_ge(S("vec_in"), 16)
            wab = three(vec("ab"), KC)
            for t in range(T):
                for k in range(KC):
                    last = mm(flat[:, 2048 + 8 * t:2048 + 8 * t + 8], HT[:, k, 128 * t:128 * t + 128],
                              wab[:, k, :], start=(k == 0), stop=(k == KC - 1))
            last.then_inc(*signal("ab_done"))
            for j in range(PIN):
                wp = three(piece(pe, j), KC)
                for pp in range(2):
                    g = 2 * j + pp
                    if g >= 4:
                        conv_free(pe, g - 4)
                    for c in range(2):
                        o = 512 * (g % 4) + 256 * c
                        for k in range(KC):
                            if g < 13:
                                last = mm(flat[:, o:o + 256],
                                          wp[:, k, 256 * pp + 128 * c:256 * pp + 128 * c + 128],
                                          HT[:, k, :], start=(k == 0), stop=(k == KC - 1))
                            else:
                                last = mm(flat[:, o:o + 256], HT[:, k, 128 * c:128 * c + 128],
                                          wp[:, k, 256:512], start=(k == 0), stop=(k == KC - 1))
                    last.then_inc(S("proj"), 1)

            scr = three(SCREP, KC)

            def ada(g, b, ks):
                wp = [three(piece(pe, FIRST["ada"] + 4 * g + j), KC) for j in range(4)]
                for k in ks:
                    for j in range(4):
                        last = mm(flat[32 * j:32 * j + 32, 512 * b:512 * b + 512], scr[:, k, :],
                                  wp[j][:, k, :], start=(k == 0), stop=(k == KC - 1))
                if k == KC - 1:
                    last.then_inc(S("ada"), 1)

            def pick(c):
                return ident[:, 32 * (c % 4):32 * (c % 4) + 1]

            def gate_rows(i):
                for h in range(2):
                    c = (4, 10)[i] + h
                    last = mm(bank(h), pick(c).broadcast_to([P, P]), three(MODR, 3)[:, c // 4, :], start=True, stop=True)
                last.then_inc(S("gtb"), 1)

            pe.wait_ge(*step("a8"))
            conv_free(pe, 11)
            mm(flat[:, 1536:1544], upto, A8, start=True, stop=True)
            mm(flat[:, 1544:1552], same, A8, start=True, stop=True).then_inc(*signal("gcol_done"))
            pe.wait_ge(S("abc"), 2)
            for m in range(M8):
                last = mm(flat[:, 2048 + 128 * m:2048 + 128 * m + 128], ABC[:, 128 * m:128 * m + 128], upto,
                          start=True, stop=True)
            last.then_inc(*signal("gb_done"))
            for m in range(M8):
                last = mm(flat[:, 3072 + 128 * m:3072 + 128 * m + 128], BBC[:, 128 * m:128 * m + 128], ident,
                          start=True, stop=True)
            last.then_inc(*signal("bb_done"))
            for i in range(2):
                pe.wait_ge(S("l2sq"), i + 1)
                if i == 0:
                    conv_free(pe, 12)
                    conv_free(pe, 13)
                else:
                    pe.wait_ge(S("gcol_in"), 1)
                for h in range(2):
                    last = mm(bank(2 * i + h), ones, (SQR if i == 0 else OT)[:, 512 * h:512 * h + 512], start=True, stop=True)
                last.then_inc(S("l2sum"), 1)
            pe.wait_ge(*step("screp"))
            pe.wait_ge(S("l2r"), 1)
            ada(0, 0, range(KC))
            pe.wait_ge(S("l2norm"), 2)
            pe.wait_ge(S("modr"), 1)
            for m in range(M8):
                t, h = divmod(m, NH)
                kt = KT[:, L * h + P * t:L * h + P * t + P]
                last = mm(flat[:, 128 * m:128 * m + 128], kt, kt, start=True, stop=True)
            last.then_inc(*signal("kk_done"))
            for m in range(M8):
                t, h = divmod(m, NH)
                last = mm(flat[:, 1024 + 128 * m:1024 + 128 * m + 128], KT[:, L * h + P * t:L * h + P * t + P],
                          QT[:, L * h + P * t:L * h + P * t + P], start=True, stop=True)
            last.then_inc(*signal("at_done"))
            pe.wait_ge(S("mlt"), 2)
            for m in range(M8):
                t, h = divmod(m, NH)
                last = nc.tensor.transpose(flat[:, 3072 + 128 * m:3072 + 128 * m + 128],
                                           KT[:, L * h + P * t:L * h + P * t + P], ident)
            last.then_inc(*signal("krow"))
            pe.wait_ge(*step("gdt"))
            for m in range(M8):
                t, h = divmod(m, NH)
                last = nc.tensor.transpose(flat[:, 2048 + 128 * m:2048 + 128 * m + 128],
                                           VT[:, L * h + P * t:L * h + P * t + P], ident)
            last.then_inc(*signal("vrow"))
            pe.wait_ge(S("krow_in"), 2)
            pe.wait_ge(S("vrow_in"), 1)
            pe.wait_ge(*step("atm"))
            for l in range(6):
                pe.wait_ge(S("cl"), l + 1)
                if l:
                    pe.wait_ge(S("xi"), 2 * l)
                for m in range(M8):
                    s = slice(128 * m, 128 * m + 128)
                    last = mm(flat[:, s], CL[:, s], XI[:, s], start=True, stop=True)
                    if m % 4 == 3:
                        last.then_inc(S("y"), 1)
                pe.wait_ge(S("yl_act"), l + 1)
                pe.wait_ge(S("yl_dve"), l + 1)
                for m in range(M8):
                    s = slice(128 * m, 128 * m + 128)
                    last = mm(flat[:, 1024 + 128 * m:1024 + 128 * m + 128], XIT[:, s], YL[:, s], start=True, stop=True)
                last.then_inc(S("xy"), 1)
                for m in range(M8):
                    s = slice(128 * m, 128 * m + 128)
                    last = mm(flat[:, 2048 + 128 * m:2048 + 128 * m + 128], YL[:, s], XIT[:, s], start=True, stop=True)
                last.then_inc(S("yx"), 1)
                if l in (1, 2):
                    ada(1, 7, range(4 * l - 4, 4 * l))
                elif l > 3:
                    ada(2, 6, range(4 * l - 16, 4 * l - 12))
            pe.wait_ge(S("xi"), 12)
            for m in range(M8):
                s = slice(128 * m, 128 * m + 128)
                last = mm(flat[:, s], XIT[:, s], VB[:, s], start=True, stop=True)
            last.then_inc(*signal("u"))
            for m in range(M8):
                s = slice(128 * m, 128 * m + 128)
                last = mm(flat[:, 1024 + 128 * m:1024 + 128 * m + 128], KB[:, s], XIT[:, s], start=True, stop=True)
            last.then_inc(*signal("w"))
            for n in range(NCH):
                t, b0 = n // 2, 64 * (n % 2)
                if n:
                    pe.wait_ge(S("state"), n)
                    pe.wait_ge(*step("wt_in"))
                    for h in range(NH):
                        m = NH * t + h
                        last = mm(flat[:, 2048 + 128 * h:2048 + 128 * h + 128], WT[:, 128 * m:128 * m + 128],
                                  ST[:, 128 * h:128 * h + 128], start=True, stop=True)
                    last.then_inc(S("ws"), 1)
                    if n > 1:
                        pe.wait_ge(S("os"), n - 1)
                    for h in range(NH):
                        m = NH * t + h
                        last = mm(flat[:, 2560 + 64 * h:2560 + 64 * h + 64], ST[:, 128 * h:128 * h + 128],
                                  QT[:, L * h + P * t + b0:L * h + P * t + b0 + 64], start=True, stop=True)
                    last.then_inc(S("qs"), 1)
                pe.wait_ge(S("vn"), n + 1)
                if n == 0:
                    pe.wait_ge(S("modr"), 3)
                if n < NCH - 1:
                    for h in range(NH):
                        m = NH * t + h
                        last = mm(flat[:, 3072 + 128 * h:3072 + 128 * h + 128], KD[b0:b0 + 64, 128 * m:128 * m + 128],
                                  VN[b0:b0 + 64, 128 * m:128 * m + 128], start=True, stop=True)
                    last.then_inc(S("kv"), 1)
                if n % 2:
                    if n > 1:
                        pe.wait_ge(S("ot"), 1)
                    for h in range(NH):
                        m = NH * t + h
                        last = mm(flat[:, 3584 + 128 * h:3584 + 128 * h + 128], VN[:, 128 * m:128 * m + 128],
                                  ATM[:, 128 * m:128 * m + 128], start=True, stop=True)
                    last.then_inc(S("av"), 1)
            pe.wait_ge(*step("osq"))
            pe.wait_ge(*step("wt_in"))
            for h in range(2):
                last = mm(bank(h), ones, XI[:, 512 * h:512 * h + 512], start=True, stop=True)
            last.then_inc(*signal("osum"))
            for hp in range(2):
                if hp:
                    pe.wait_ge(S("sb_lom"), 1)
                for i in range(2):
                    r = slice(64 * i, 64 * i + 64)
                    q = SBQ[r, L * hp:L * hp + L]
                    mm(flat[:, 1024 + 512 * i:1024 + 512 * i + 256], SBK[r, L * hp:L * hp + 128], q,
                       start=True, stop=True)
                    last = mm(flat[:, 1024 + 512 * i + 256:1024 + 512 * i + 384], SBK[r, L * hp + 128:L * hp + 256],
                              q[:, 128:256], start=True, stop=True)
                last.then_inc(S("sb_z"), 1)
                if hp == 0:
                    pe.wait_ge(S("ot"), 2)
                    modr = three(MODR, 3)
                    for i, c0 in enumerate((0, 2, 6, 8)):
                        for k in range(KC):
                            c = c0 + k // 4
                            last = mm(flat[:, 3584 + 8 * i + k:3584 + 8 * i + k + 1],
                                      modr[:, c // 4, 128 * (k % 4):128 * (k % 4) + 128], pick(c), start=True, stop=True)
                    last.then_inc(*signal("modc"))
                    pe.wait_ge(*step("orinv"))
                else:
                    pe.wait_ge(S("gtb_in"), 1)
                gate_rows(hp)
                pe.wait_ge(S("sb_lom"), hp + 1)
                if hp:
                    pe.wait_ge(S("sb_lb"), 1)
                for i in range(2):
                    o = 2048 + 512 * i
                    lom = SB1[:, 384 * i:384 * i + 384]
                    mm(flat[:, o:o + 256], after, lom[:, 0:256], start=True, stop=False)
                    mm(flat[:, o + 128:o + 256], ones, lom[:, 256:384], start=False, stop=True)
                    last = mm(flat[:, o + 256:o + 384], after, lom[:, 256:384], start=True, stop=True)
                last.then_inc(S("sb_tail"), 1)
                pe.wait_ge(S("sb_a"), hp + 1)
                for i in range(2):
                    h = 2 * hp + i
                    o = 3072 + 256 * hp
                    a = SB2[:, 384 * i:384 * i + 384]
                    mm(flat[64 * i:64 * i + 64, o:o + 256], SBV[:, 64 * h:64 * h + 64], a[:, 0:256],
                       start=True, stop=False)
                    last = mm(flat[64 * i:64 * i + 64, o + 128:o + 256], SBV[:, 256 + 64 * h:256 + 64 * h + 64],
                              a[:, 256:384], start=False, stop=True)
                last.then_inc(S("sb_o"), 1)
                pe.wait_ge(S("sb_y"), hp + 1)
            pe.wait_ge(S("gtb_in"), 2)
            pe.wait_ge(*step("y_sc"))
            pe.wait_ge(*step("y_gdn"))
            pe_rows(FIRST["mo"], KC, YT, "mo_done")
            pe_norm(2)
            hT_ready(pe, 2)

            def up(n, wp, uses):
                for pp in range(2):
                    b = 4 + 2 * (uses % 2) + pp
                    for c in range(2):
                        o = 512 * b + 256 * c
                        for k in range(KC):
                            last = mm(flat[:, o:o + 256], wp[:, k, 256 * pp + 128 * c:256 * pp + 128 * c + 128],
                                      HT[:, k, :], start=(k == 0), stop=(k == KC - 1))
                last.then_inc(S("up"), 1)

            for j in range(UPEEL):
                wp = three(piece(pe, FIRST["up"] + j), KC)
                if j >= 2:
                    pe.wait_ge(S("fconv_done"), 2 * (j - 1))
                up(j, wp, j)
            with pe.Fori(0, (PUP - UPEEL) // NSLOT1) as i:
                for j in range(NSLOT1):
                    n0 = FIRST["up"] + UPEEL + j
                    s = n0 % NSLOT1
                    pe.wait_ge(S(f"slot{s}_loaded"), 16 * i + 16 * taken(n0))
                    pe.wait_ge(S("fconv_done"), 8 * i + 2 * (UPEEL + j - 1))
                    up(j, three(ring[:, s, :], KC), UPEEL + j)
            pe.wait_ge(S("gt"), PUP)
            pe_rows(FIRST["dn"], 2 * PUP, three(GT, 22), "down_done")
            pe_norm(3)
            hT_ready(pe, 3)
            for j in range(PIN2):
                wp = three(piece(pe, FIRST["in2"] + j), KC)
                for pp in range(2):
                    g = 2 * j + pp
                    b = 4 + g % 4
                    if g >= 4:
                        pe.wait_ge(S("proj2_in"), g - 3)
                    if g < 8:
                        for c in range(2):
                            o = 512 * b + 256 * c
                            for k in range(KC):
                                last = mm(flat[:, o:o + 256], wp[:, k, 256 * pp + 128 * c:256 * pp + 128 * c + 128],
                                          HT[:, k, :], start=(k == 0), stop=(k == KC - 1))
                    else:
                        for k in range(KC):
                            last = mm(bank(b), HT[:, k, 128 * pp:128 * pp + 128], wp[:, k, :],
                                      start=(k == 0), stop=(k == KC - 1))
                    last.then_inc(S("proj2"), 1)
            pe.wait_ge(*step("lamp"))
            mm(flat[:, 0:2], ones[0:64, :], lam2[0:64, 0:2], start=True, stop=True).then_inc(*signal("lams"))
            pe.wait_ge(*step("nlam"))
            pe.wait_ge(S("proj2_in"), 12)

            def scores(u):
                q, k = (DQ, DK) if u < 8 else (NQ, NK)
                c, r = (u % 8) // 2, slice(64 * (u % 2), 64 * (u % 2) + 64)
                if u >= 2:
                    pe.wait_ge(S("sc_in"), u - 1)
                for t in range(T):
                    last = mm(flat[:, 512 * (u % 2) + 256 * t:512 * (u % 2) + 256 * t + 256],
                              q[r, L * c + P * t:L * c + P * t + P], k[r, L * c:L * c + L], start=True, stop=True)
                last.then_inc(S("scores"), 1)

            def out_of(v):
                pe.wait_ge(S("pa"), v + 1)
                if v >= 2:
                    pe.wait_ge(S("pt"), v - 1)
                for kt in range(T):
                    for qt in range(T):
                        o = 1024 + 512 * (v % 2) + 256 * kt + 128 * qt
                        last = nc.tensor.transpose(flat[:, o:o + 128],
                                                   PA[v % 2][:, 256 * qt + 128 * kt:256 * qt + 128 * kt + 128], ident)
                last.then_inc(S("pat"), 1)
                pe.wait_ge(S("pt"), v + 1)
                if v < 4:
                    dst, vv = flat[:, 2048 + 256 * v:2048 + 256 * v + 256], [DV[:, 512 * kt + 128 * v:512 * kt + 128 * v + 128] for kt in range(T)]
                else:
                    n = v - 4
                    o = 3072 + 256 * (n // 2)
                    dst = flat[64 * (n % 2):64 * (n % 2) + 64, o:o + 256]
                    vv = [NV[:, 512 * kt + 64 * n:512 * kt + 64 * n + 64] for kt in range(T)]
                for kt in range(T):
                    last = mm(dst, vv[kt], PT[v % 2][:, 256 * kt:256 * kt + 256], start=(kt == 0), stop=(kt == T - 1))
                last.then_inc(S("ov"), 1)

            v = 0
            for u in range(16):
                scores(u)
                if u < 8:
                    if u >= 3 and u % 2:
                        out_of(v)
                        v += 1
                elif u >= 9:
                    out_of(v)
                    v += 1
            while v < 12:
                out_of(v)
                v += 1
            pe.wait_ge(*step("dsq"))
            for h in range(2):
                last = mm(bank(h), ones, DSQ[:, 512 * h:512 * h + 512], start=True, stop=True)
            last.then_inc(*signal("dsum"))
            pe.wait_ge(*step("y_diff"))
            pe.wait_ge(*step("y_nat"))
            pe_rows(FIRST["out"], KC, YT, "out_done")
            pe_norm(4)
            hT_ready(pe, 4)
            wr = three(vec("router"), KC)
            for t in range(T):
                for k in range(KC):
                    last = mm(flat[:, 2048 + 32 * t:2048 + 32 * t + 32], HT[:, k, 128 * t:128 * t + 128], wr[:, k, :],
                              start=(k == 0), stop=(k == KC - 1))
            last.then_inc(*signal("lg"))
            for t in range(T):
                for k in range(KC):
                    last = nc.tensor.transpose(flat[:, 1024 * t + 128 * k:1024 * t + 128 * k + 128],
                                               HT[:, k, 128 * t:128 * t + 128], ident)
                last.then_inc(S("h2r"), 1)
            pe.wait_ge(*step("mask"))
            mm(flat[:, 2560:2592], before, MASK[:, 0, :], start=True, stop=True)
            mm(flat[:, 2592:2624], before, MASK[:, 1, :], start=True, stop=False)
            mm(flat[:, 2592:2624], ones, MASK[:, 0, :], start=False, stop=True)
            for t in range(T):
                last = mm(flat[0:32, 2624:2625], MASK[:, t, :], ones[:, 0:1], start=(t == 0), stop=(t == T - 1))
            last.then_inc(*signal("pos"))
            pe.wait_ge(*step("cnr"))
            mm(flat[0:32, 3072:3073], before[0:32, 0:32], CNR[0:32], start=True, stop=True)
            mm(flat[0:1, 3073:3105], CNR[0:32], before[0:32, 0:32], start=True, stop=True)
            mm(flat[0:1, 3105:3137], CNR[0:32], ident[0:32, 0:32], start=True, stop=True)
            mm(flat[0:1, 3137:3138], CNR[0:32], ones[0:32, 0:1], start=True, stop=True).then_inc(*signal("cum"))
            pe.wait_ge(S("gate"), 2)
            for i, a in enumerate((PM, GATE)):
                for t in range(T):
                    o = 3584 + 256 * i + 128 * t
                    last = nc.tensor.transpose(flat[0:32, o:o + 128], a[:, t, :], ident)
            last.then_inc(*signal("pmt"))
            pe.wait_ge(S("pmt_in"), 1)
            pe.wait_ge(S("oh"), 2)
            for t in range(T):
                o = 2048 + NPMAX * t
                mm(flat[:, o:o + NPMAX], PMT[0:32, 128 * t:128 * t + 128], OH[0:32], start=True, stop=False)
                mm(flat[:, o:o + NPMAX], ones[0:32, :], RM[0:32], start=False, stop=True)
            for t in range(T):
                o = 2048 + 128 + NPMAX * t
                last = mm(flat[:, o:o + NPMAX], GTT[0:32, 128 * t:128 * t + 128], OH[0:32], start=True, stop=True)
            last.then_inc(*signal("pp"))
            pe.wait_ge(S("h2r_in"), 2)
            pe.wait_ge(S("b_in"), 32)
            for t in range(T):
                for h in range(2):
                    mm(bank(2 * t + h), GTT[0:32, 128 * t:128 * t + 128], B2[0:32, 512 * h:512 * h + 512],
                       start=True, stop=False, skip_group_check=True)

            def gather():
                for t in range(T):
                    for q in range(4):
                        last = mm(flat[32 * q:32 * q + 32, 3072:3328], SEL[:, t, :], H2R[:, t, 256 * q:256 * q + 256],
                                  start=(t == 0), stop=(t == T - 1))
                last.then_inc(S("g"), 1)

            def gather_transpose():
                for b in range(2):
                    last = nc.tensor.transpose(flat[:, 3584 + 128 * b:3584 + 128 * b + 128], GS[:, 128 * b:128 * b + 128], ident)
                last.then_inc(S("h"), 1)

            def scatter(quarters, signal, release=False):
                for t in range(T):
                    for q in quarters:
                        r = slice(32 * q, 32 * q + 32)
                        o = 1024 * t + 256 * q
                        last = mm(flat[:, o:o + 256], SGT[r, 128 * t:128 * t + 128], YS[r, :], start=False, stop=False,
                                  skip_group_check=True)
                        if release and t == 0 and q == quarters[0]:
                            last.then_inc(S("wused"), 1)
                last.then_inc(S(signal), 1)

            def up1(loaded, release):
                for kk in range(4):
                    wp = loaded(kk)
                    for b in range(2):
                        for q in range(4):
                            last = mm(flat[32 * q:32 * q + 32, 2048:2560], XG[:, b, 32 * kk:32 * kk + 32],
                                      wp[:, 2048 * b + 512 * q:2048 * b + 512 * q + 512],
                                      start=(kk == 0 and b == 0), stop=(kk == 3 and b == 1))
                        if kk == 0 and b == 0:
                            for q in range(4):
                                mm(flat[32 * q:32 * q + 32, 2048:2560], OHB[0:NE, :], B1[0:NE, 512 * q:512 * q + 512],
                                   start=False, stop=False)
                    if release and kk < 3:
                        last.then_inc(S("wused"), 1)
                last.then_inc(S("w1"), 1)

            def down1(loaded, release):
                for c in range(KC):
                    if c % 4 == 0:
                        wp = loaded(4 + c // 4)
                    for q in range(4):
                        last = mm(flat[32 * q:32 * q + 32, 3072:3328],
                                  AT[:, 128 * (c % 2) + 32 * (c // 2):128 * (c % 2) + 32 * (c // 2) + 32],
                                  wp[:, 1024 * (c % 4) + 256 * q:1024 * (c % 4) + 256 * q + 256],
                                  start=(c == 0), stop=(c == KC - 1))
                    if release and c == 3:
                        last.then_inc(S("wused"), 1)
                last.then_inc(S("w2"), 1)
                if release:
                    mm(flat[0:1, 2560:2561], ones[0:1, 0:1], ones[0:1, 0:1], start=True, stop=True).then_inc(S("wused"), 1)

            def one_pass(p, loaded, release):
                pe.wait_ge(S("xg"), p + 1)
                pe.wait_ge(S("ohb"), p + 1)
                up1(loaded, release)
                pe.wait_ge(S("y_in"), p + 1)
                pe.wait_ge(S("sgt_in"), p + 1)
                scatter((0, 2), "scat_a", release)
                pe.wait_ge(S("sel"), p + 2)
                gather()
                pe.wait_ge(S("scat_a"), p + 1)
                scatter((1, 3), "scat")
                pe.wait_ge(S("sg"), p + 1)
                for t in range(T):
                    last = nc.tensor.transpose(flat[:, 3584 + 128 * t:3584 + 128 * t + 128], SG[:, t, :], ident)
                last.then_inc(S("sgtp"), 1)
                pe.wait_ge(S("act"), p + 1)
                for b in range(2):
                    last = nc.tensor.transpose(flat[:, 2560 + 128 * b:2560 + 128 * b + 128], HID[:, 128 * b:128 * b + 128], ident)
                last.then_inc(S("at"), 1)
                pe.wait_ge(S("g_in"), p + 2)
                pe.wait_ge(S("sgt_in"), p + 2)
                gather_transpose()
                pe.wait_ge(S("at_in"), p + 1)
                down1(loaded, release)

            pe.wait_ge(S("sel"), 1)
            pe.wait_ge(*step("cum_in"))
            gather()
            pe.wait_ge(S("g_in"), 1)
            pe.wait_ge(S("pmt_in"), 1)
            gather_transpose()
            with pe.Fori(0, NE // ESTEP) as i:
                for j in range(ESTEP):
                    def loaded(r, j=j):
                        n = 6 * j + r
                        s = n % NSLOT
                        pe.wait_ge(S(f"slot{s}_loaded"), 16 * (EPIECES // NSLOT) * i + 16 * (slot_base[s] + n // NSLOT + 1))
                        return ring[:, s, :]

                    first = pe.value_load(passes[0:1, bass.ds(ESTEP * i + j, 1)], min_val=0, max_val=NPMAX - 1)
                    more = pe.value_load(passes[0:1, bass.ds(ESTEP * i + j + NE, 1)], min_val=0, max_val=L // CAP - 1)
                    with pe.If(more > 0):
                        with pe.Fori(0, more) as r:
                            one_pass(first + r, loaded, False)
                    one_pass(first + more, loaded, True)
            n_passes = pe.value_load(passes[0:1, 64:65], min_val=NE, max_val=NPMAX - 1)
            pe.wait_ge(S("y_in"), n_passes + 1)
            pe.wait_ge(S("sgt_in"), n_passes + 1)
            scatter((0, 2), "scat_a")
            pe.wait_ge(S("scat_a"), n_passes + 1)
            scatter((1, 3), "scat")

        def linked(eng, name):
            n = [0]

            def link(ins):
                n[0] += 1
                ins.then_inc(S(name), 1)
                eng.wait_ge(S(name), n[0])
            return link

        def act_square(i):
            a = nc.scalar
            if i == 1:
                a.wait_ge(S("x_in"), 16)
            else:
                a.wait_ge(S(f"x{i}"), T)
            for t in range(T):
                a.activation(XN[:, t, :], X[:, t, :], ACT.Square, accum_out=ssq[:, t:t + 1]).then_inc(S("ssq"), 1)

        def act_norm(i, scale, shift=None):
            a = nc.scalar
            act_square(i)
            a.wait_ge(S("rinv"), NORMS.index(i) + 1)
            a.activation(rstd, mean, ACT.Sqrt).then_inc(S("rstd"), 1)
            a.wait_ge(S("vec_in"), 16)
            for b in (1, 3):
                a.wait_ge(S("xT"), 4 * (i - 1) + b + 1)
                for k in (2 * b, 2 * b + 1):
                    sh = 0.0 if shift is None else shift[:, k:k + 1]
                    last = a.activation(HT[:, k, :], flat[:, 256 * k:256 * k + 256], ACT.Identity,
                                        bias=sh, scale=scale[:, k:k + 1])
                last.then_inc(S("hT_act"), 1)

        def dve_norm(link, i, scale, shift=None, normalised=None):
            v = nc.vector
            v.wait_ge(S("ssq"), SQUARES[i])
            link(v.tensor_scalar(mean, ssq[:, 0:2], 1.0 / D, EPS, ALU.mult, ALU.add))
            v.reciprocal(mean, mean).then_inc(S("rinv"), 1)
            v.wait_ge(S("rstd"), NORMS.index(i) + 1)
            for t in range(T):
                v.tensor_scalar(XN[:, t, :], X[:, t, :], rstd[:, t:t + 1], None, ALU.mult).then_inc(S("xn"), 1)
            v.wait_ge(S("vec_in"), 16)
            for b in (0, 2):
                v.wait_ge(S("xT"), 4 * (i - 1) + b + 1)
                for k in (2 * b, 2 * b + 1):
                    if shift is None:
                        last = v.tensor_scalar(HT[:, k, :], flat[:, 256 * k:256 * k + 256], scale[:, k:k + 1], None, ALU.mult)
                    else:
                        last = v.tensor_scalar(HT[:, k, :], flat[:, 256 * k:256 * k + 256], scale[:, k:k + 1],
                                               shift[:, k:k + 1], ALU.mult, ALU.add)
                last.then_inc(S("hT_dve"), 1)

        @block.scalar
        def _(a):
            link = linked(a, "act_chain")
            f = a.activation
            act_norm(1, vec("norm_mix"))
            gconv = three(vec("gconv"), 12)
            for j in range(3):
                dst = (KT, QT, VT)[j]
                for pp in range(2):
                    g = 2 * j + pp
                    a.wait_ge(S("proj"), g + 1)
                    for c in range(2):
                        ch = 2 * pp + c
                        last = f(dst[:, L * ch:L * ch + L], flat[:, 512 * (g % 4) + 256 * c:512 * (g % 4) + 256 * c + 256],
                                 ACT.Copy, scale=gconv[:, 4 * j + ch, 3:4])
                    last.then_inc(S("gconv_first"), 1)
            for g in (6, 7):
                a.wait_ge(S("proj"), g + 1)
                f(GZ[:, 512 * (g - 6):512 * (g - 6) + 512], bank(g % 4), ACT.Silu).then_inc(S("proj_act"), 1)
            for j in range(3):
                dst = (KT, QT, VT)[j]
                a.wait_ge(S("gconv_done"), 2 * j + 2)
                f(dst, dst, ACT.Silu).then_inc(S("gsilu"), 1)
            a.wait_ge(S("proj"), 9)
            f(SCP, bank(0), ACT.Copy).then_inc(S("proj_act"), 1)
            a.wait_ge(S("proj"), 11)
            f(SCB, bank(2), ACT.Copy).then_inc(S("proj_act"), 1)
            a.wait_ge(S("proj"), 12)
            f(SBQ, bank(3), ACT.Copy, scale=0.125).then_inc(S("proj_act"), 1)
            a.wait_ge(S("proj"), 13)
            f(SBK, bank(0), ACT.Copy).then_inc(S("proj_act"), 1)
            a.wait_ge(S("proj"), 14)
            f(SBV, bank(1), ACT.Copy).then_inc(S("proj_act"), 1)
            link(f(silc, vec("c"), ACT.Silu))
            a.wait_ge(S("gu"), 3)
            link(f(v8, v8, ACT.Exp, scale=-1.0))
            f(v8, v8, ACT.Ln, bias=1.0).then_inc(S("gl"), 1)
            f(ea4, vec("alog"), ACT.Exp).then_inc(S("gl"), 1)
            f(e8, e8, ACT.Exp, scale=-1.0).then_inc(S("gl"), 1)
            a.wait_ge(S("gsilu"), 2)
            f(SQR, KT, ACT.Square).then_inc(S("l2sq"), 1)
            f(OT, QT, ACT.Square).then_inc(S("l2sq"), 1)
            a.wait_ge(S("l2r"), 1)
            f(SQR, SQR, ACT.Sqrt).then_inc(S("l2s"), 1)
            a.wait_ge(S("l2r"), 2)
            f(OT, OT, ACT.Sqrt, scale=1.0 / P).then_inc(S("l2s"), 1)
            a.wait_ge(S("gcol_in"), 1)
            f(EGC, GCOL, ACT.Exp).then_inc(S("egc"), 1)
            a.wait_ge(*step("egl_d"))
            f(EGL, EGL, ACT.Exp).then_inc(S("egc"), 1)
            a.wait_ge(*step("gb_done"))
            f(EG, bank(4, 2), ACT.Exp).then_inc(*signal("eg"))
            a.wait_ge(*step("gdt"))
            f(DT, DT, ACT.Exp).then_inc(*signal("dt"))
            a.wait_ge(*step("krow"))
            for m in range(M8):
                last = f(KD[:, 128 * m:128 * m + 128], flat[:, 3072 + 128 * m:3072 + 128 * m + 128], ACT.Copy,
                         scale=EGL[:, m:m + 1])
            last.then_inc(S("krow_in"), 1)
            for l in range(6):
                a.wait_ge(S("y"), 2 * l + 1)
                if l:
                    a.wait_ge(S("yx"), l)
                f(YL[:, 0:512], bank(0), ACT.Copy).then_inc(S("yl_act"), 1)
            a.wait_ge(*step("w"))
            f(WT, bank(2, 2), ACT.Copy).then_inc(*signal("wt_in"))
            for n in range(1, NCH):
                a.wait_ge(S("qs"), n)
                o3 = OS.rearrange("p (h c) -> p h c", h=NH)[:, :, 64 * n:64 * n + 64]
                f(o3, flat[:, 2560:2816].rearrange("p (h c) -> p h c", h=NH), ACT.Copy).then_inc(S("os"), 1)
            a.wait_ge(S("ot"), 2)
            f(XI, OT, ACT.Square).then_inc(*signal("osq"))
            a.wait_ge(*step("orinv"))
            f(XI, XI, ACT.Sqrt).then_inc(*signal("orstd"))
            for hp in range(2):
                a.wait_ge(S("sb_z"), hp + 1)
                if hp:
                    a.wait_ge(S("sb_o"), 1)
                z3 = flat[:, 1024:2048].rearrange("p (i c) -> p i c", i=2)[:, :, 0:384]
                link(f(three(SB1, 2), z3, ACT.Abs))
                link(f(SB1, SB1, ACT.Exp, scale=-1.0))
                f(SB1, SB1, ACT.Ln, bias=1.0).then_inc(S("sb_ln"), 1)
                a.wait_ge(S("sb_lb"), hp + 1)
                f(SB2, SB2, ACT.Exp).then_inc(S("sb_exp"), 1)
                a.wait_ge(S("sb_o"), hp + 1)
                f(YT[:, 6 + hp, :], flat[:, 3072 + 256 * hp:3072 + 256 * hp + 256], ACT.Copy).then_inc(S("sb_y"), 1)
            a.wait_ge(S("sb_y"), 2)
            a.wait_ge(S("gtb_in"), 2)
            act_norm(2, vec("norm_ffn"))
            fc3 = three(vec("fconv"), PUP)

            for j in range(PUP):
                a.wait_ge(S("up"), j + 1)
                o = 2048 + 1024 * (j % 2)
                uc = (UC, UC2)[j % 2]
                if j >= 2:
                    a.wait_ge(S("gt"), j - 1)
                for c in range(4):
                    last = f(uc[:, 256 * c:256 * c + 256], flat[:, o + 256 * c:o + 256 * c + 256], ACT.Copy,
                             scale=fc3[:, j, 3 * c + 2:3 * c + 3])
                last.then_inc(S("fconv_first"), 1)
                a.wait_ge(S("fconv_done"), 2 * j + 2)
                f(uc[:, 0:512], uc[:, 0:512], ACT.Silu).then_inc(S("usilu"), 1)
            a.wait_ge(S("xf"), T)
            for t in range(T):
                f(XN[:, t, :], X[:, t, :], ACT.Square, accum_out=ssq[:, t:t + 1]).then_inc(S("ssq"), 1)
            a.wait_ge(S("rinv"), NORMS.index("f") + 1)
            f(rstd, mean, ACT.Sqrt).then_inc(S("rstd"), 1)
            act_norm(3, GW1, MODC[:, 0:8])
            for g in range(12):
                a.wait_ge(S("proj2"), g + 1)
                dst = (DQ, DK, NQ, NK, DV, NV)[g // 2][:, 512 * (g % 2):512 * (g % 2) + 512]
                f(dst, bank(4 + g % 4), ACT.Copy, scale=0.125 if g // 2 in (0, 2) else 1.0).then_inc(S("proj2_in"), 1)
            a.wait_ge(*step("lams"))
            f(lam2[:, 2:4], flat[:, 0:2], ACT.Exp).then_inc(*signal("elam"))

            def probs(u):
                s = three(SC[u % 2], T)
                a.wait_ge(S("nmax"), u + 1)
                for t in range(T):
                    last = f(s[:, t, :], s[:, t, :], ACT.Exp, bias=nmx[:, 2 * (u % 2) + t:2 * (u % 2) + t + 1],
                             accum_out=sme[:, 2 * (u % 2) + t:2 * (u % 2) + t + 1])
                    last.then_inc(S("probs"), 1)

            def evac(v):
                a.wait_ge(S("pat"), v + 1)
                if v >= 2:
                    a.wait_ge(S("ov"), v - 1)
                f(PT[v % 2], bank(2 + v % 2), ACT.Copy).then_inc(S("pt"), 1)

            v = 0
            for u in range(16):
                probs(u)
                if (u < 8 and u >= 3 and u % 2) or u >= 9:
                    evac(v)
                    v += 1
            while v < 12:
                evac(v)
                v += 1
            a.wait_ge(S("ov"), 12)
            f(DSQ, bank(4, 2), ACT.Square).then_inc(*signal("dsq"))
            f(DO, bank(4, 2), ACT.Copy).then_inc(*signal("do"))
            f(YT[:, 4:8, :], three(bank(6, 2), 4), ACT.Copy).then_inc(*signal("y_nat"))
            a.wait_ge(*step("drinv"))
            f(DRS, DRS, ACT.Sqrt).then_inc(*signal("drstd"))
            a.wait_ge(S("out_done"), 4)
            for t in range(T):
                for h in range(2):
                    f(XN[:, t, 512 * h:512 * h + 512], bank(2 * t + h), ACT.Square,
                      accum_out=ssq[:, 2 * t + h:2 * t + h + 1]).then_inc(S("ssq"), 1)
            a.wait_ge(S("rinv"), NORMS.index("m") + 1)
            f(rstd, mean, ACT.Sqrt).then_inc(S("rstd"), 1)
            act_norm(4, GW2, MODC[:, 16:24])
            a.wait_ge(*step("lgs"))
            f(EE, EE, ACT.Exp).then_inc(*signal("ee"))
            a.wait_ge(S("h2r"), 2)
            f(H2R[:, 1, :], bank(2, 2), ACT.Copy).then_inc(S("h2r_in"), 1)
            a.wait_ge(S("h"), 1)
            f(XG.rearrange("p a b -> p (a b)"), flat[:, 3584:3840], ACT.Copy).then_inc(S("xg"), 1)
            a.wait_ge(*step("cum_in"))
            n_passes = a.value_load(passes[0:1, 64:65], min_val=NE, max_val=NPMAX - 1)
            with a.Fori(0, n_passes) as p:
                a.wait_ge(S("glu"), p + 1)
                f(SIG, GLU, ACT.Sigmoid, scale=1.702).then_inc(S("sig"), 1)
                a.wait_ge(S("sgtp"), p + 1)
                a.wait_ge(S("scat"), p + 1)
                f(SGT, flat[:, 3584:3840], ACT.Copy).then_inc(S("sgt_in"), 1)
                a.wait_ge(S("at"), p + 1)
                f(AT, flat[:, 2560:2816], ACT.Copy).then_inc(S("at_in"), 1)
                a.wait_ge(S("h"), p + 2)
                f(XG.rearrange("p a b -> p (a b)"), flat[:, 3584:3840], ACT.Copy).then_inc(S("xg"), 1)
                a.wait_ge(S("w2"), p + 1)
                f(YS, flat[:, 3072:3328], ACT.Copy).then_inc(S("y_in"), 1)
            a.wait_ge(S("scat"), n_passes + 1)
            for t in range(T):
                for h in range(2):
                    f(XN[:, t, 512 * h:512 * h + 512], bank(2 * t + h), ACT.Square,
                      accum_out=ssq[:, 2 * t + h:2 * t + h + 1]).then_inc(S("ssq"), 1)
            a.wait_ge(S("rinv"), NORMS.index("e") + 1)
            f(rstd, mean, ACT.Sqrt).then_inc(S("rstd"), 1)

        @block.vector
        def _(v):
            link = linked(v, "dve_chain")
            tt, ts, stt = v.tensor_tensor, v.tensor_scalar, v.scalar_tensor_tensor
            dve_norm(link, 1, vec("norm_mix"))
            ab = flat[:, 2048:2064].rearrange("p (t c) -> p t c", t=T)
            v.wait_ge(*step("ab_done"))
            link(tt(three(u8, T), ab[:, :, 0:4], vec("dtb").unsqueeze(1).broadcast_to([P, T, 4]), ALU.add))
            link(v.tensor_copy(three(e8, T), ab[:, :, 4:8]))
            link(stt(v8, u8, -1.0, u8, ALU.mult, ALU.max))
            ts(u8, u8, 0.0, None, ALU.max).then_inc(S("gu"), 3)
            gconv = three(vec("gconv"), 12)
            for j in range(3):
                dst = (KT, QT, VT)[j]
                for pp in range(2):
                    g = 2 * j + pp
                    v.wait_ge(S("gconv_first"), g + 1)
                    for tap in (2, 1, 0):
                        sh = 3 - tap
                        for c in range(2):
                            ch = 2 * pp + c
                            o = 512 * (g % 4) + 256 * c
                            d = dst[:, L * ch + sh:L * ch + L]
                            last = stt(d, flat[:, o:o + 256 - sh], gconv[:, 4 * j + ch, tap:tap + 1], d, ALU.mult, ALU.add)
                            if tap:
                                link(last)
                    last.then_inc(S("gconv_done"), 1)
                    v.wait_ge(S("gconv_done"), g + 1)
            v.wait_ge(S("proj"), 10)
            v.wait_ge(S("proj_act"), 3)
            tt(SCP, bank(1), SCP, ALU.mult).then_inc(*signal("sc_prod"))
            v.wait_ge(S("gl"), 3)
            link(tt(u8, u8, v8, ALU.add))
            stt(three(A8, T), three(u8, T), -1.0, ea4.unsqueeze(1).broadcast_to([P, T, 4]), ALU.mult, ALU.mult).then_inc(*signal("a8"))
            link(ts(e8, e8, 1.0, None, ALU.add))
            link(v.reciprocal(BET, e8))
            v.wait_ge(*step("a8"))
            v.tensor_copy(three(ABC, M8), A8.unsqueeze(2).broadcast_to([P, M8, P])).then_inc(S("abc"), 1)
            v.tensor_copy(three(BBC, M8), BET.unsqueeze(2).broadcast_to([P, M8, P])).then_inc(S("abc"), 1)
            v.wait_ge(S("act_chain"), 1)
            v.wait_ge(S("proj"), 14)
            v.tensor_copy(three(SCREP, KC), silc.unsqueeze(2).broadcast_to([P, KC, 32])).then_inc(*signal("screp"))
            modr = three(MODR, 3)

            def modulation(g, b):
                v.wait_ge(S("bada_in"), 16)
                v.wait_ge(S("ada"), g + 1)
                tt(modr[:, g, :], modr[:, g, :], bank(b), ALU.add).then_inc(S("modr"), 1)

            for i in range(2):
                r = (SQR, OT)[i]
                v.wait_ge(S("l2sum"), i + 1)
                link(ts(r, bank(2 * i, 2), EPS, None, ALU.add))
                v.reciprocal(r, r).then_inc(S("l2r"), 1)
                if i == 0:
                    v.wait_ge(*step("gcol_done"))
                    v.tensor_copy(GCOL, flat[:, 1536:1544])
                    v.tensor_copy(GLAST, flat[:, 1544:1552]).then_inc(S("gcol_in"), 1)
                    v.wait_ge(S("gcol_in"), 1)
                    tt(EGL, GLAST, GCOL, ALU.subtract).then_inc(*signal("egl_d"))
            for i in range(2):
                v.wait_ge(S("l2s"), i + 1)
                d = (KT, QT)[i]
                tt(d, d, (SQR, OT)[i], ALU.mult).then_inc(S("l2norm"), 1)
            modulation(0, 0)
            v.wait_ge(S("egc"), 1)
            link(tt(BEG, BET, EGC, ALU.mult))
            v.wait_ge(*step("eg"))
            v.wait_ge(S("l2norm"), 2)
            for m in range(M8):
                last = ts(DT[:, 128 * m:128 * m + 128], flat[:, 2048 + 128 * m:2048 + 128 * m + 128],
                          GCOL[:, m:m + 1], 0.0, ALU.subtract, ALU.min)
            last.then_inc(*signal("gdt"))
            v.wait_ge(*step("dt"))
            v.wait_ge(*step("kk_done"))
            tt(MLT, bank(0, 2), DT, ALU.mult).then_inc(S("mlt"), 1)
            v.wait_ge(*step("bb_done"))
            v.wait_ge(S("mlt"), 1)
            tt(MLT, MLT, bank(6, 2), ALU.mult).then_inc(S("mlt"), 1)
            v.wait_ge(*step("at_done"))
            link(tt(ATM, bank(2, 2), DT, ALU.mult))
            tt(three(ATM, M8), three(ATM, M8), upto.unsqueeze(1).broadcast_to([P, M8, P]), ALU.mult).then_inc(*signal("atm"))
            qv, ev = QT.rearrange("p (h t c) -> p h t c", h=NH, t=T), EG.rearrange("p (t h c) -> p h t c", h=NH, t=T)
            for h in range(NH):
                last = tt(qv[:, h], qv[:, h], ev[:, h], ALU.mult)
            v.wait_ge(S("krow_in"), 1)
            for m in range(M8):
                last = ts(KB[:, 128 * m:128 * m + 128], flat[:, 3072 + 128 * m:3072 + 128 * m + 128],
                          BEG[:, m:m + 1], None, ALU.mult)
            last.then_inc(S("krow_in"), 1)
            v.wait_ge(*step("vrow"))
            for m in range(M8):
                last = ts(VB[:, 128 * m:128 * m + 128], flat[:, 2048 + 128 * m:2048 + 128 * m + 128],
                          BET[:, m:m + 1], None, ALU.mult)
            last.then_inc(S("vrow_in"), 1)
            v.tensor_copy(three(XI, M8), ident.unsqueeze(1).broadcast_to([P, M8, P]))
            link(v.tensor_copy(three(XIT, M8), ident.unsqueeze(1).broadcast_to([P, M8, P])))
            v.wait_ge(S("mlt"), 2)
            for l in range(6):
                if l:
                    v.wait_ge(S("y"), 2 * l)
                tt(three(CL, M8), three(MLT, M8), level[:, l, :].unsqueeze(1).broadcast_to([P, M8, P]), ALU.mult).then_inc(S("cl"), 1)
                v.wait_ge(S("y"), 2 * l + 2)
                v.tensor_copy(YL[:, 512:1024], bank(1)).then_inc(S("yl_dve"), 1)
                v.wait_ge(S("xy"), l + 1)
                v.wait_ge(S("yx"), l + 1)
                tt(XI, XI, bank(2, 2), ALU.add).then_inc(S("xi"), 1)
                tt(XIT, XIT, bank(4, 2), ALU.add).then_inc(S("xi"), 1)
                v.wait_ge(S("xi"), 2 * l + 2)
                if l == 3:
                    modulation(1, 7)
            modulation(2, 6)
            v.wait_ge(*step("u"))
            link(v.tensor_copy(U, bank(0, 2)))
            eg4 = EG.rearrange("p (m c) -> p m c", m=M8)
            sc3, sp3, sy3, sb3 = (three(z, 2) for z in (vec("sconv"), SCP, SCY, SCB))
            v.wait_ge(*step("sc_prod"))
            for tap in (2, 1, 0):
                sh = 2 - tap
                for c in range(2):
                    w = sc3[:, c, tap:tap + 1]
                    if tap == 2:
                        link(ts(sy3[:, c, :], sp3[:, c, :], w, None, ALU.mult))
                    else:
                        link(stt(sy3[:, c, sh:L], sp3[:, c, 0:L - sh], w, sy3[:, c, sh:L], ALU.mult, ALU.add))
            v.wait_ge(S("proj_act"), 4)
            tt(YT[:, 0:2, :], sy3, sb3, ALU.mult).then_inc(*signal("y_sc"))
            link(v.memset(OS.rearrange("p (h c) -> p h c", h=NH)[:, :, 0:64], 0.0))
            for n in range(NCH):
                t, b0 = n // 2, 64 * (n % 2)
                cols = slice(512 * t, 512 * t + 512)
                rows_ = slice(b0, b0 + 64)
                if n == 0:
                    v.tensor_copy(VN[rows_, cols], U[rows_, cols]).then_inc(S("vn"), 1)
                else:
                    v.wait_ge(S("ws"), n)
                    stt(VN[rows_, cols], flat[rows_, 2048:2560], -1.0, U[rows_, cols], ALU.mult, ALU.add).then_inc(S("vn"), 1)
                if n < NCH - 1:
                    v.wait_ge(S("kv"), n + 1)
                    if n:
                        v.wait_ge(S("qs"), n)
                    if n == 0:
                        v.tensor_copy(ST, bank(6)).then_inc(S("state"), 1)
                    else:
                        v.wait_ge(S("state"), n)
                        for h in range(NH):
                            s = slice(128 * h, 128 * h + 128)
                            last = stt(ST[:, s], ST[:, s], eg4[:, NH * t + h, b0 + 63:b0 + 64], flat[:, 3072 + 128 * h:3072 + 128 * h + 128],
                                       ALU.mult, ALU.add)
                        last.then_inc(S("state"), 1)
                if n % 2:
                    v.wait_ge(S("av"), t + 1)
                    v.wait_ge(S("os"), n)
                    dst = OT.rearrange("p (h c) -> p h c", h=NH)[:, :, 128 * t:128 * t + 128]
                    tt(dst, three(bank(7), NH), OS.rearrange("p (h c) -> p h c", h=NH)[:, :, 128 * t:128 * t + 128],
                       ALU.add).then_inc(S("ot"), 1)
            v.wait_ge(*step("osum"))
            link(ts(XI, bank(0, 2), 1.0 / P, EPS, ALU.mult, ALU.add))
            v.reciprocal(XI, XI).then_inc(*signal("orinv"))
            v.wait_ge(S("proj_act"), 2)
            v.wait_ge(S("ot"), 2)
            link(stt(OT, OT, vec("gnorm"), GZ, ALU.mult, ALU.mult))
            v.wait_ge(*step("orstd"))
            tt(YT[:, 2:6, :], three(OT, NH), three(XI, NH), ALU.mult).then_inc(*signal("y_gdn"))
            z3 = flat[:, 1024:2048].rearrange("p (i c) -> p i c", i=2)[:, :, 0:384]
            tail3 = flat[:, 2048:3072].rearrange("p (i c) -> p i c", i=2)[:, :, 0:384]
            s1, s2 = three(SB1, 2), three(SB2, 2)
            mask = before.unsqueeze(1).broadcast_to([P, 2, P])
            for hp in range(2):
                v.wait_ge(S("sb_ln"), hp + 1)
                link(stt(s2, z3, 0.0, s1, ALU.min, ALU.subtract))
                link(stt(s1, z3, -1.0, s2, ALU.mult, ALU.add))
                tt(s1[:, :, 0:128], s1[:, :, 0:128], mask, ALU.mult)
                tt(s1[:, :, 256:384], s1[:, :, 256:384], mask, ALU.mult).then_inc(S("sb_lom"), 1)
                v.wait_ge(S("sb_tail"), hp + 1)
                tt(s2, s2, tail3, ALU.add).then_inc(S("sb_lb"), 1)
                v.wait_ge(S("sb_exp"), hp + 1)
                tt(s2[:, :, 0:128], s2[:, :, 0:128], mask, ALU.mult)
                tt(s2[:, :, 256:384], s2[:, :, 256:384], mask, ALU.mult).then_inc(S("sb_a"), 1)
                if hp == 0:
                    v.wait_ge(*step("modc"))
                    link(v.tensor_copy(MODC, flat[:, 3584:3616]))
                    link(stt(GW1, MODC[:, 8:16], 1.0, vec("pre_mix"), ALU.add, ALU.mult))
                    link(stt(GW2, MODC[:, 24:32], 1.0, vec("pre_ffn"), ALU.add, ALU.mult))
                    v.wait_ge(S("rows_in"), 16)
                v.wait_ge(S("gtb"), hp + 1)
                g = (G1B, G2B)[hp]
                tt(g, g, bank(0, 2), ALU.mult).then_inc(S("gtb_in"), 1)

            def residual(done, signal, n):
                for t in range(T):
                    for h in range(2):
                        v.wait_ge(S(done), 2 * t + h + 1)
                        last = tt(X[:, t, 512 * h:512 * h + 512], X[:, t, 512 * h:512 * h + 512], bank(2 * t + h), ALU.add)
                    last.then_inc(S(signal), 1)

            residual("mo_done", "x2", 1)
            dve_norm(link, 2, vec("norm_ffn"))
            fc3 = three(vec("fconv"), PUP)
            gt3 = three(GT, 22)
            for j in range(PUP):
                uc = (UC, UC2)[j % 2]
                v.wait_ge(S("fconv_first"), j + 1)
                o = 2048 + 1024 * (j % 2)
                for tap in (1, 0):
                    sh = 2 - tap
                    for c in range(4):
                        last = stt(uc[:, 256 * c + sh:256 * c + 256], flat[:, o + 256 * c:o + 256 * c + 256 - sh],
                                   fc3[:, j, 3 * c + tap:3 * c + tap + 1], uc[:, 256 * c + sh:256 * c + 256], ALU.mult, ALU.add)
                    last.then_inc(S("fconv_done"), 1)
                    v.wait_ge(S("fconv_done"), 2 * j + 2 - tap)
                v.wait_ge(S("usilu"), j + 1)
                tt(gt3[:, 2 * j:2 * j + 2, :], three(uc[:, 0:512], 2), three(uc[:, 512:1024], 2), ALU.mult).then_inc(S("gt"), 1)
            residual("down_done", "xf", 2)
            v.wait_ge(S("ssq"), SQUARES["f"])
            link(ts(mean, ssq[:, 0:2], 1.0 / D, EPS, ALU.mult, ALU.add))
            v.reciprocal(mean, mean).then_inc(S("rinv"), 1)
            v.wait_ge(S("rstd"), NORMS.index("f") + 1)
            for t in range(T):
                stt(X[:, t, :], X[:, t, :], rstd[:, t:t + 1], WFIN, ALU.mult, ALU.mult).then_inc(S("x3"), 1)
            v.wait_ge(S("x3"), T)
            dve_norm(link, 3, GW1, MODC[:, 0:8])
            lam = vec("lam")
            tt(lam2[0:64, 0:2], lam[0:64, 0:2], lam[0:64, 2:4], ALU.mult).then_inc(*signal("lamp"))
            v.wait_ge(*step("elam"))
            link(tt(nlam, lam2[:, 3:4], lam2[:, 2:3], ALU.subtract))
            ts(nlam, nlam, -0.2, None, ALU.add).then_inc(*signal("nlam"))
            v.wait_ge(*step("nlam"))
            v.wait_ge(S("natb_in"), 16)
            nb = NB.rearrange("p (r w) -> p r w", w=64)
            link(tt(nb, nb, const("window").unsqueeze(1).broadcast_to([P, 64, 64]), ALU.add))

            def softmax(u):
                s = SC[u % 2]
                s3 = three(s, T)
                z = bank(u % 2)
                v.wait_ge(S("scores"), u + 1)
                if u >= 10:
                    v.wait_ge(S("pa"), u - 5)
                elif u >= 3:
                    v.wait_ge(S("pa"), (u - 1) // 2)
                if u < 8:
                    slope = 2.0 ** (-8.0 * (u // 2 + 1) / NH)
                    stt(s, const("dist"), -slope, z, ALU.mult, ALU.add).then_inc(S("sc_in"), 1)
                else:
                    tt(s, NB[:, 512 * (u - 8):512 * (u - 8) + 512], z, ALU.add).then_inc(S("sc_in"), 1)
                v.wait_ge(S("sc_in"), u + 1)
                v.tensor_reduce(nmx[:, 2 * (u % 2):2 * (u % 2) + 2], s3, AX_X, ALU.max, negate=True).then_inc(S("nmax"), 1)

            def weigh(u):
                v.wait_ge(S("probs"), 2 * u + 2)
                r = rcs[:, 2 * (u % 2):2 * (u % 2) + 2]
                link(v.reciprocal(r, sme[:, 2 * (u % 2):2 * (u % 2) + 2]))
                s3 = three(SC[u % 2], T)
                w = u // 2 if u < 8 else u - 4
                pa3 = three(PA[w % 2], T)
                if w >= 2:
                    v.wait_ge(S("pat"), w - 1)
                if u < 8 and u % 2:
                    link(ts(r, r, nlam, None, ALU.mult))
                    for t in range(T):
                        last = stt(pa3[:, t, :], s3[:, t, :], r[:, t:t + 1], pa3[:, t, :], ALU.mult, ALU.add)
                    last.then_inc(S("pa"), 1)
                    v.wait_ge(S("pa"), w + 1)
                elif u < 8:
                    for t in range(T):
                        link(ts(pa3[:, t, :], s3[:, t, :], r[:, t:t + 1], None, ALU.mult))
                else:
                    for t in range(T):
                        last = ts(pa3[:, t, :], s3[:, t, :], r[:, t:t + 1], None, ALU.mult)
                    last.then_inc(S("pa"), 1)

            softmax(0)
            for u in range(1, 16):
                softmax(u)
                weigh(u - 1)
            weigh(15)
            v.wait_ge(*step("dsum"))
            link(ts(DRS, bank(0, 2), 1.0 / P, EPS, ALU.mult, ALU.add))
            v.reciprocal(DRS, DRS).then_inc(*signal("drinv"))
            v.wait_ge(*step("do"))
            link(ts(DO, DO, vec("subln"), 1.0 - 0.2, ALU.mult, ALU.mult))
            v.wait_ge(*step("drstd"))
            tt(YT[:, 0:4, :], three(DO, NH), three(DRS, NH), ALU.mult).then_inc(*signal("y_diff"))

            def gated(which, ready, gate, signal):
                v.wait_ge(S("ssq"), SQUARES[which])
                s4 = ssq.rearrange("p (t h) -> p t h", t=T)
                link(tt(mean.unsqueeze(2), s4[:, :, 0:1], s4[:, :, 1:2], ALU.add))
                link(ts(mean, mean, 1.0 / D, EPS, ALU.mult, ALU.add))
                v.reciprocal(mean, mean).then_inc(S("rinv"), 1)
                v.wait_ge(S("rstd"), NORMS.index(which) + 1)
                for t in range(T):
                    for h in range(2):
                        hs = slice(512 * h, 512 * h + 512)
                        link(stt(XN[:, t, hs], bank(2 * t + h), rstd[:, t:t + 1], gate[:, hs], ALU.mult, ALU.mult))
                    tt(X[:, t, :], X[:, t, :], XN[:, t, :], ALU.add).then_inc(S(signal), 1)

            gated("m", None, G1B, "x4")
            v.wait_ge(S("x4"), T)
            dve_norm(link, 4, GW2, MODC[:, 16:24])
            v.memset(IR[:, :, 4:8], -3.0e38)
            link(v.memset(LX[:, :, 32:36], -3.0e38))
            v.wait_ge(*step("lg"))
            link(tt(LG, three(flat[:, 2048:2112], T), vec("brt").unsqueeze(1).broadcast_to([P, T, NE]), ALU.add))
            link(v.tensor_copy(LX[:, :, 0:32], LG))
            for t in range(T):
                link(v.max(V8[:, t, :], LG[:, t, :]))
            link(v.tensor_copy(IR[:, :, 0:4], V8[:, :, 0:4]))
            for t in range(T):
                link(v.match_replace(MR[:, t, 0:36], IR[:, t, :], LX[:, t, 0:36], 3.0e38))
            tt(MASK, MR[:, :, 0:32], LG, ALU.not_equal).then_inc(*signal("mask"))
            tt(EE, LG, V8[:, :, 0:1].broadcast_to([P, T, NE]), ALU.subtract).then_inc(*signal("lgs"))
            v.wait_ge(*step("mask"))
            v.wait_ge(*step("ee"))
            link(tt(EE, EE, MASK, ALU.mult))
            link(v.tensor_reduce(GSUM, EE, AX_X, ALU.add))
            link(v.reciprocal(GSUM, GSUM))
            tt(GATE, EE, GSUM.unsqueeze(2).broadcast_to([P, T, NE]), ALU.mult).then_inc(S("gate"), 1)
            v.wait_ge(*step("pos"))
            link(stt(PM, MASK, -1000.0, three(flat[:, 2560:2624], T), ALU.mult, ALU.add))
            ts(PM, PM, 1000.0, None, ALU.add).then_inc(S("gate"), 1)
            cnt = flat[0:32, 2624:2625]
            link(ts(CNR[0:32], cnt, float(CAP), 1.0, ALU.is_gt, ALU.add))
            for i in range(2, L // CAP):
                link(stt(CNR[0:32], cnt, float(CAP * i), CNR[0:32], ALU.is_gt, ALU.add))
            ts(CNR[0:32], CNR[0:32], 0.0, None, ALU.add).then_inc(*signal("cnr"))
            v.wait_ge(*step("cum"))
            v.wait_ge(*step("cnr"))
            link(v.tensor_copy(CCE[0:32], flat[0:32, 3072:3073]))
            v.tensor_copy(passes[0:1, 0:32], flat[0:1, 3073:3105])
            ts(passes[0:1, 32:64], flat[0:1, 3105:3137], -1.0, None, ALU.add)
            v.tensor_copy(passes[0:1, 64:65], flat[0:1, 3137:3138]).then_inc(*signal("cum_in"))
            link(tt(CCI[0:32], CCE[0:32], CNR[0:32], ALU.add))
            count = const("count")[0:32, :]
            link(ts(OH[0:32], count, CCI[0:32], None, ALU.is_lt))
            stt(OH[0:32], count, CCE[0:32], OH[0:32], ALU.is_ge, ALU.mult).then_inc(S("oh"), 1)
            link(ts(RM[0:32], count, CCE[0:32], -float(CAP), ALU.subtract, ALU.mult))
            v.wait_ge(S("oh"), 1)
            tt(RM[0:32], RM[0:32], OH[0:32], ALU.mult).then_inc(S("oh"), 1)
            v.wait_ge(*step("pmt"))
            link(v.tensor_copy(PMT[0:32], flat[0:32, 3584:3840]))
            v.tensor_copy(GTT[0:32], flat[0:32, 3840:4096]).then_inc(S("pmt_in"), 1)
            v.wait_ge(S("h2r"), 1)
            v.tensor_copy(H2R[:, 0, :], bank(0, 2)).then_inc(S("h2r_in"), 1)
            v.wait_ge(*step("pp"))
            link(v.tensor_copy(PP, three(flat[:, 2048:2048 + T * NPMAX], T)))
            link(v.tensor_copy(GP, three(flat[:, 2176:2176 + T * NPMAX], T)))
            v.memset(SGT, 0.0).then_inc(S("sgt_in"), 1)
            v.memset(YS, 0.0).then_inc(S("y_in"), 1)
            slot = const("slot")

            def select(p):
                for t in range(T):
                    last = ts(SEL[:, t, :], slot[:, 0:CAP], PP[:, t, bass.ds(p, 1)], None, ALU.is_equal)
                last.then_inc(S("sel"), 1)

            def select_gated(p):
                v.tensor_copy(OHB[0:NE, :], OH[0:NE, bass.ds(p, 1)].broadcast_to([NE, CAP])).then_inc(S("ohb"), 1)
                for t in range(T):
                    last = ts(SG[:, t, :], slot, PP[:, t, bass.ds(p, 1)], GP[:, t, bass.ds(p, 1)], ALU.is_equal, ALU.mult)
                last.then_inc(S("sg"), 1)

            def swiglu(p):
                v.wait_ge(S("w1"), p + 1)
                ts(GLU, flat[:, 2048:2304], 7.0, None, ALU.min).then_inc(S("glu"), 1)
                ts(LIN, flat[:, 2304:2560], 7.0, -7.0, ALU.min, ALU.max).then_inc(S("lin"), 1)
                v.wait_ge(S("lin"), p + 1)
                v.wait_ge(S("glu"), p + 1)
                stt(HID, LIN, 1.0, GLU, ALU.add, ALU.mult).then_inc(S("hid"), 1)
                v.wait_ge(S("hid"), p + 1)
                v.wait_ge(S("sig"), p + 1)
                tt(HID, HID, SIG, ALU.mult).then_inc(S("act"), 1)

            select(0)
            select_gated(0)
            v.wait_ge(S("g"), 1)
            v.tensor_copy(GS, flat[:, 3072:3328]).then_inc(S("g_in"), 1)
            v.wait_ge(*step("cum_in"))
            n_passes = v.value_load(passes[0:1, 64:65], min_val=NE, max_val=NPMAX - 1)
            with v.Fori(0, n_passes) as p:
                v.wait_ge(S("g"), p + 1)
                select(p + 1)
                swiglu(p)
                v.wait_ge(S("g"), p + 2)
                v.wait_ge(S("h"), p + 1)
                v.tensor_copy(GS, flat[:, 3072:3328]).then_inc(S("g_in"), 1)
                v.wait_ge(S("sgtp"), p + 1)
                select_gated(p + 1)
            gated("e", None, G2B, "x5")



def _constants():
    c = np.zeros((P, NCONST), np.float32)
    i, j = np.arange(P)[:, None], np.arange(P)[None, :]

    def put(name, a):
        o, w = CO[name]
        c[:, o:o + w] = a

    chunk = (i // GCH) == (j // GCH)
    put("ident", i == j)
    put("ones", 1.0)
    put("before", i < j)
    put("after", i > j)
    put("slot", j % CAP)
    put("row", np.broadcast_to(i, (P, 64)))
    put("count", np.broadcast_to(np.arange(NPMAX)[None], (P, NPMAX)))
    put("upto", (i <= j) & chunk)
    put("same", chunk)
    lv = []
    for l in range(6):
        s = 1 << l
        lv.append(-1.0 * (((i // (2 * s)) == (j // (2 * s))) & ((i // s) % 2 == 0) & ((j // s) % 2 == 1)))
    put("level", np.concatenate(lv, 1))
    put("dist", np.concatenate([np.abs(np.arange(L)[None] - (P * t + i)) for t in range(T)], 1))
    col = np.arange(P)[:, None] % 64
    start = np.clip(col - 8, 0, 48)
    cc = np.arange(64)[None]
    put("window", np.where((cc >= start) & (cc < start + 16), 0.0, -BIG))
    return c


def _layout(inputs):
    g = {k: np.asarray(v) for k, v in inputs.items()}

    def cols(v):
        return v.reshape(-1, P).T

    vec = np.zeros((P, NVEC), np.float32)

    def put(name, a):
        o, w = VO[name]
        vec[:a.shape[0], o:o + w] = a

    put("norm_mix", cols(g["w_norm_mix"][0]))
    put("norm_ffn", cols(g["w_norm_ffn"][0]))
    put("pre_mix", cols(g["g_pre_mix_2"][0]))
    put("pre_ffn", cols(g["g_pre_ffn_2"][0]))
    put("sconv", g["w_sconv"][0].reshape(3, 2, P).transpose(2, 1, 0).reshape(P, 6))
    gc = g["w_gdn_conv"][0].reshape(4, 3, 4, P)[:, [1, 0, 2]]
    put("gconv", gc.transpose(3, 1, 2, 0).reshape(P, 48))
    put("gnorm", g["w_gdn_norm"][0][:, None])
    put("subln", g["g_subln_2"][0][:, None])
    put("lam", np.stack([g[n][0] for n in ("lam_q1_2", "lam_q2_2", "lam_k1_2", "lam_k2_2")], 1))
    put("c", cols(g["c_2"][0]))
    win = g["w_mix_in"][0]
    put("ab", win[:, 2816:2824].reshape(KC, P, 8).transpose(1, 0, 2).reshape(P, 64))
    put("alog", np.broadcast_to(g["gdn_a_log"], (P, 4)))
    put("dtb", np.broadcast_to(g["gdn_dt_bias"], (P, 4)))
    put("brt", np.broadcast_to(g["b_router_2"], (P, NE)))
    fc = g["w_ffn_conv"][0].reshape(3, 2, PUP, 2, P)
    put("fconv", fc.transpose(4, 2, 1, 3, 0).reshape(P, PUP * 12))
    put("router", g["w_router_2"][0].reshape(KC, P, NE).transpose(1, 0, 2).reshape(P, KC * NE))

    def by_columns(w):
        return w.reshape(KC, P, -1, 512).transpose(2, 1, 0, 3).reshape(-1, P, NPIECE)

    def by_rows(w):
        return w.reshape(-1, 4, P, 1024).transpose(0, 2, 1, 3).reshape(-1, P, NPIECE)

    def sl(a, n):
        return win[:, a:a + n]

    order = np.concatenate([sl(768 + 512, 512), sl(768, 512), sl(768 + 1024, 512), sl(768 + 1536, 512),
                            sl(256, 512), sl(0, 256), sl(2824, 256), sl(2824 + 256, 512)], 1)
    up = g["w_ffn_up"][0].reshape(D, 2, PUP, 256).transpose(0, 2, 1, 3).reshape(D, 2 * DFF)
    down = np.concatenate([g["w_ffn_down"][0], np.zeros((256, D), np.float32)])
    w_in2 = g["w_in_2"][0]
    two = np.concatenate([w_in2[:, 0:1024], w_in2[:, 1536:2560], w_in2[:, 1024:1536], w_in2[:, 2560:3072]], 1)
    stream = np.concatenate([by_columns(order), by_columns(g["w_ada_2"][0]), by_rows(g["w_mix_out"][0]),
                             by_columns(up), by_rows(down), by_columns(two), by_rows(g["w_out_2"][0])])
    assert stream.shape[0] == NSTREAM
    bada = np.broadcast_to(g["b_ada_2"][0].reshape(3, 4, 1, 512).transpose(1, 2, 0, 3), (4, 32, 3, 512))
    rows = np.stack([g["w_norm_final"], g["g_post_mix_2"][0], g["g_post_ffn_2"][0]]).reshape(1, 3072)
    r, c = np.arange(4), np.arange(64)
    dr = (r[None, :] - r[:, None]) + 7
    dc = np.clip(c[None, :] - c[:, None], -15, 15) + 15
    nb = g["nat_rpb_2"][0][:, dr[:, None, :, None], dc[None, :, None, :]].reshape(8, T, P, L)
    w1 = g["w1_2"][0].reshape(NE, 4, 2, P, 4, 256, 2).transpose(0, 1, 3, 2, 4, 6, 5).reshape(NE * 4, P, NPIECE)
    w2 = g["w2_2"][0].reshape(NE, 2, 4, P, 1024).transpose(0, 1, 3, 2, 4).reshape(NE * 2, P, NPIECE)
    b1 = g["b1_2"][0].reshape(NE, 4, 256, 2).transpose(0, 1, 3, 2).reshape(NE, 2048)
    return {
        "consts": _constants(), "vecs": vec, "stream": stream, "bada": bada.reshape(P, 1536),
        "rows": np.broadcast_to(rows, (P, 3072)), "natb": nb.transpose(2, 0, 1, 3).reshape(P, 4096),
        "w1": w1, "w2": w2, "b1": b1, "b2": g["b2_2"][0],
        "x": g["x"][0].reshape(T, P, D).transpose(1, 0, 2).reshape(P, T * D),
    }


def kernel(**inputs):
    import concourse.bacc as bacc
    from concourse.bass_utils import run_bass_kernel_spmd

    nc = bacc.Bacc("TRN2", target_bir_lowering=False, num_devices=1)
    arrays, args = {}, {}
    for name, a in _layout(inputs).items():
        arrays["in_" + name] = np.ascontiguousarray(a)
        args[name] = nc.dram_tensor("in_" + name, a.shape, mybir.dt.from_np(a.dtype), kind="ExternalInput").ap()
    args["out"] = nc.dram_tensor("out_0", (P, T * D), F32, kind="ExternalOutput").ap()
    first_block_and_moe(nc, **args)
    got = run_bass_kernel_spmd(nc, [arrays], core_ids=[0]).results[0]["out_0"]
    return got.reshape(P, T, D).transpose(1, 0, 2).reshape(1, L, D)
```

```python
from contextlib import ExitStack

import numpy as np
import concourse.bass as bass
from concourse import mybir

F32 = mybir.dt.float32
I32 = mybir.dt.int32
BF16 = mybir.dt.bfloat16
F32R = mybir.dt.float32r
ALU = mybir.AluOpType
ACT = mybir.ActivationFunctionType
AX_X = mybir.AxisListType.X

P = 128
D = 1024
L = 256
KC = D // P
T = L // P
DFF = 2816
NH = 4
M8 = T * NH
GCH = 64
NCH = L // GCH
NE = 32
TOPK = 4
CAP = 32
EPS = 1e-6
BIG = 1.0e30
NPIECE = 4096
PIN, PADA, PMO, PUP, PDN, PIN2, POUT = 7, 12, 2, 11, 6, 6, 2
FIRST = dict(inp=0)
FIRST["ada"] = FIRST["inp"] + PIN
FIRST["mo"] = FIRST["ada"] + PADA
FIRST["up"] = FIRST["mo"] + PMO
FIRST["dn"] = FIRST["up"] + PUP
FIRST["in2"] = FIRST["dn"] + PDN
FIRST["out"] = FIRST["in2"] + PIN2
NSTREAM = FIRST["out"] + POUT
NSLOT1, NLOW, NSLOT = 4, 8, 9
NPMAX = 64

CO, _at = {}, 0
for _n, _w in (("ident", P), ("ones", P), ("before", P), ("slot", P), ("row", 64), ("count", NPMAX),
               ("upto", P), ("same", P), ("after", P), ("level", 6 * P), ("dist", 2 * L),
               ("window", 64)):
    CO[_n] = (_at, _w)
    _at += _w
NCONST = _at
VO, _at = {}, 0
for _n, _w in (("norm_mix", 8), ("norm_ffn", 8), ("pre_mix", 8), ("pre_ffn", 8), ("sconv", 6),
               ("gconv", 48), ("gnorm", 1), ("subln", 1), ("lam", 4), ("c", 8), ("ab", 64),
               ("alog", 4), ("dtb", 4), ("brt", NE), ("fconv", PUP * 12), ("router", KC * NE)):
    VO[_n] = (_at, _w)
    _at += _w
NVEC = _at


def first_block_and_moe(nc, consts, vecs, stream, bada, rows, natb, w1, w2, b1, b2, x, out):
    ctx = ExitStack()
    with ctx:
        TOTAL = 53100
        LOW = NLOW * NPIECE
        low = ctx.enter_context(nc.sbuf_tensor("low", [P, LOW], F32))
        high_part = ctx.enter_context(nc.sbuf_tensor("high_part", [P, TOTAL - LOW], F32))
        mem_at = nc.sbuf_base - 4 * TOTAL
        flat = ctx.enter_context(nc.psum_tensor("acc", [P, 8 * 512], F32))

        sems = {}

        def S(name):
            if name not in sems:
                sems[name] = ctx.enter_context(nc.semaphore(name))
            return sems[name]

        NORMS = [1, 2, "f", 3, "m", 4, "e"]
        SQUARES = dict(zip(NORMS, np.cumsum([T, T, T, T, 2 * T, T, 2 * T]).tolist()))

        STEPS = dict(
            pe_step=("ab_done gcol_done gb_done bb_done kk_done at_done krow vrow u w osum modc lams dsum lg pos cum pmt pp"),
            act_step=("eg dt wt_in osq orstd elam dsq do y_nat drstd ee"),
            dve_step=("sc_prod a8 screp egl_d gdt atm y_sc orinv y_gdn lamp nlam drinv y_diff mask lgs cnr cum_in"))
        STEPS = {engine: names.split() for engine, names in STEPS.items()}
        signalled = {engine: [] for engine in STEPS}

        def engine_of(name):
            return [engine for engine, names in STEPS.items() if name in names][0]

        def step(name):
            engine = engine_of(name)
            return S(engine), STEPS[engine].index(name) + 1

        def signal(name):
            engine = engine_of(name)
            signalled[engine].append(name)
            assert signalled[engine] == STEPS[engine][:len(signalled[engine])], name
            return S(engine), 1

        def at(off, n):
            assert off >= LOW or off + n <= LOW
            return low[:, off:off + n] if off < LOW else high_part[:, off - LOW:off - LOW + n]

        def bank(b, n=1):
            return flat[:, 512 * b:512 * (b + n)]

        def three(ap, a):
            return ap.rearrange("p (a b) -> p a b", a=a)

        ring = three(at(0, NLOW * NPIECE), NLOW)
        WORK = NSLOT1 * NPIECE
        base = NLOW * NPIECE
        X = three(at(base, 2048), T)
        XN = three(at(base + 2048, 2048), T)
        HT = three(at(base + 4096, 2048), KC)
        YT = three(at(base + 6144, 2048), KC)
        CST, VEC = base + 8192, base + 8192 + NCONST
        BC = VEC + NVEC
        EX = BC + 3072
        assert TOTAL - EX >= 5632 + 150
        WFIN, G1B, G2B = (at(BC + 1024 * i, 1024) for i in range(3))

        def const(name):
            o, w = CO[name]
            return at(CST + o, w)

        def vec(name):
            o, w = VO[name]
            return at(VEC + o, w)

        ident, ones, before, after = const("ident"), const("ones"), const("before"), const("after")
        upto, same = const("upto"), const("same")
        level = three(const("level"), 6)

        def W(i, n=1024):
            return at(WORK + 1024 * i, n)

        def E(i, n=1024, o=0):
            return at(EX + 1024 * i + o, n)

        SM = EX + 5632
        tiny = [SM]

        def small(n):
            r = at(tiny[0], n)
            tiny[0] += n
            assert tiny[0] <= TOTAL
            return r

        ssq, mean, rstd = small(4), small(2), small(2)
        A8, BET, GCOL, GLAST, EGC, EGL, BEG = (small(8) for _ in range(7))
        u8, v8, e8 = small(8), small(8), small(8)
        ea4 = small(4)
        MODC = small(32)
        GW1, GW2 = small(8), small(8)
        lam2, nlam = small(4), small(1)
        nmx, sme, rcs = small(4), small(4), small(4)
        silc = small(8)

        KT, QT, VT, GZ, ABC, BBC, EG, DT, MLT, ATM, XI, XIT, KB, KD, VB, WT = (W(i) for i in range(16))
        YL, CL, OT, U, VN = ABC, BBC, DT, XI, E(0)
        SBQ, SBK, SBV, SCP, SCB, SCY = (E(1 + i // 2, 512, 512 * (i % 2)) for i in range(6))
        SQR = E(4)
        OS = E(4)
        ST = E(5, 512)
        SB1 = at(base + 4096, 768)
        SB2 = at(base + 4096 + 768, 768)
        MODR = at(base + 2048, 1536)
        SCREP = at(base + 4096 + 1536, 256)
        UC = W(6)
        UC2 = W(7)
        DQ, DK, NQ, NK, DV, NV = (W(i) for i in range(6))
        NB = W(6, 4096)
        SC = [W(10, 512), at(WORK + 10240 + 512, 512)]
        PA = [W(11, 512), at(WORK + 11 * 1024 + 512, 512)]
        PT = [W(12, 512), at(WORK + 12 * 1024 + 512, 512)]
        DO = W(13)
        DSQ = W(14)
        DRS = W(15)

        def r32(name, off, n):
            return nc.alloc_sbuf_tensor_at(name, [P, n], F32R, offset=mem_at + 4 * off)[:, :]

        HI = [r32(f"w_hi{i}", WORK + 8192 + NPIECE * i, NPIECE) for i in range(2)]
        LO = [r32(f"w_lo{s}", NPIECE * s, NPIECE) for s in range(NSLOT1)]
        XHI, XLO = three(r32("x_hi", base + 6144, 2048), KC), three(r32("x_lo", base + 4096, 2048), KC)
        GTHI, GTLO = r32("gt_hi", WORK, 22 * L), r32("gt_lo", EX, 22 * L)
        WAB = [r32("ab_hi", EX, 64), r32("ab_lo", EX + 64, 64)]
        SPLIT = [n for part, count in (("inp", PIN), ("up", PUP), ("dn", PDN), ("in2", PIN2))
                 for n in range(FIRST[part], FIRST[part] + count)]

        def slot_of(n):
            s = n % NSLOT
            return ring[:, s, :] if s < NLOW else at(base + 4096, NPIECE)

        B1P = at(EX, 1024).bitcast(BF16)
        B1 = at(EX + 2048, 2048)
        tmp = [EX + 1024, EX + 5632]

        def temp(n):
            tmp[0] += n
            assert tmp[0] <= tmp[1]
            return at(tmp[0] - n, n)

        LG, MASK, EE, GATE, PM = (three(temp(64), T) for _ in range(5))
        LX, MR = three(temp(80), T), three(temp(80), T)
        V8, IR = three(temp(16), T), three(temp(16), T)
        GSUM, CNR, CCE, CCI, CT1 = temp(2), temp(1), temp(1), temp(1), temp(1)
        OH, RM = temp(NPMAX), temp(NPMAX)
        PP, GP = three(temp(T * NPMAX), T), three(temp(T * NPMAX), T)
        B2 = at(tmp[0], 1024)
        GLU, LIN, SIG, HID, AT = (temp(256) for _ in range(5))
        YS, GS, XG = temp(256), temp(256), three(temp(256), 2)
        SEL, SG, SGT = three(temp(T * CAP), T), three(temp(256), T), temp(256)
        OHB = temp(CAP // 2).bitcast(BF16)
        PMT, GTT = temp(256), temp(256)
        passes = ctx.enter_context(nc.sbuf_tensor("passes", [1, 72], I32))
        H2R = XN
        slot_base = [len([n for n in range(NSTREAM) if n % NSLOT1 == s]) if s < NSLOT1 else 0 for s in range(NSLOT)]
        ESTEP = 3
        EPIECES = 6 * ESTEP
        NTURN = NE // ESTEP
        assert EPIECES % NSLOT == 0

        block = ctx.enter_context(nc.Block())

        def taken(n, slots=NSLOT1):
            return n // slots + 1

        UPEEL = 3
        assert (FIRST["up"] + UPEEL) % NSLOT1 == 0 and (PUP - UPEEL) % NSLOT1 == 0

        def piece(eng, n):
            eng.wait_ge(S(f"slot{n % NSLOT1}_loaded"), 16 * taken(n))
            return ring[:, n % NSLOT1, :]

        def used(n):
            for part, one, ends in (("out", "out_k", "out_done"), ("in2", "proj2", None), ("dn", "down_k", "down_done"),
                                    ("up", "up", None), ("mo", "mo_k", "mo_done"), ("ada", "ada", None), ("inp", "proj", None)):
                if n >= FIRST[part]:
                    j = n - FIRST[part]
                    if part in ("inp", "in2"):
                        return S(one), 2 * j + 2
                    if part == "ada":
                        return S(one), j // 4 + 1
                    if part == "up":
                        return S(one), j + 1
                    last = {"mo": PMO, "dn": PDN, "out": POUT}[part] - 1
                    return (S(ends), 4) if j == last else (S(one), j + 1)

        @block.sync
        def _(sp):
            sp.dma_start(at(base, 2048), x).then_inc(S("x_in"), 16)
            sp.dma_start(at(CST, NCONST), consts).then_inc(S("const_in"), 16)
            sp.dma_start(at(VEC, NVEC), vecs).then_inc(S("vec_in"), 16)

            def load(n):
                if n >= NSLOT1:
                    sp.wait_ge(*used(n - NSLOT1))
                sp.dma_start(ring[:, n % NSLOT1, :], stream[n]).then_inc(S(f"slot{n % NSLOT1}_loaded"), 16)

            for n in range(FIRST["ada"]):
                load(n)
            sp.dma_start(at(BC, 3072), rows).then_inc(S("rows_in"), 16)
            sp.wait_ge(S("xT"), 4)
            sp.dma_start(MODR, bada).then_inc(S("bada_in"), 16)
            for n in range(FIRST["ada"], FIRST["in2"] + 4):
                load(n)
            for n in range(FIRST["in2"] + 4, NSTREAM):
                load(n)
            sp.wait_ge(S("proj2"), 2 * PIN2)
            sp.dma_start(NB, natb).then_inc(S("natb_in"), 16)
            for part in range(3):
                sp.dma_start(B1[NE * part:NE * part + NE, :], b1).then_inc(S("b1_in"), 16)

            def expert_piece(i, n):
                e, r = divmod(n, 6)
                src = w1[bass.ds(4 * ESTEP * i + 4 * e + r, 1)] if r < 4 else w2[bass.ds(2 * ESTEP * i + 2 * e + r - 4, 1)]
                sp.dma_start(slot_of(n), src.rearrange("a p n -> (a p) n"))\
                  .then_inc(S(f"slot{n % NSLOT}_loaded"), 16)

            early = [s for s in range(NSLOT1) if (s - NSTREAM) % NSLOT1 < NSLOT1 - POUT]
            for n in early + list(range(NSLOT1, NLOW)) + [s for s in range(NSLOT1) if s not in early]:
                if n < NSLOT1:
                    sp.wait_ge(*used(NSTREAM - NSLOT1 + (n - NSTREAM) % NSLOT1))
                elif n == NSLOT1:
                    sp.wait_ge(*step("y_diff"))
                    sp.wait_ge(*step("y_nat"))
                expert_piece(0, n)
            sp.wait_ge(S("x4"), T)
            sp.wait_ge(S("b1_parts"), 7)
            sp.dma_start(B2[0:NE, :], b2).then_inc(S("b_in"), 16)
            sp.wait_ge(S("h2r"), T)
            expert_piece(0, NLOW)
            with sp.Fori(0, NTURN) as i:
                for j in range(EPIECES):
                    sp.wait_ge(S("wused"), EPIECES * i + j + 1)
                    expert_piece(i, NSLOT + j)
            for n in range(NSLOT + NTURN * EPIECES, NE * 6):
                sp.wait_ge(S("wused"), n - NSLOT + 1)
                expert_piece(0, n)
            for t in range(T):
                sp.wait_ge(S("x5"), t + 1)
                sp.dma_start(out[:, 1024 * t:1024 * t + 1024], X[:, t, :]).then_inc(S("stored"), 16)
            sp.wait_ge(S("stored"), 32)

        def pe_norm(i):
            pe = nc.tensor
            pe.wait_ge(S("xn"), T * i)
            if i == 1:
                pe.wait_ge(S("const_in"), 16)
            for k in range(KC):
                for t in range(T):
                    o = 512 * (k // 2) + 256 * (k % 2) + 128 * t
                    last = nc.tensor.transpose(flat[:, o:o + 128], XN[:, t, 128 * k:128 * k + 128], ident)
                if k % 2:
                    last.then_inc(S("xT"), 1)

        def hT_ready(pe, i):
            pe.wait_ge(S("hT_dve"), 2 * i)
            pe.wait_ge(S("hT_act"), 2 * i)

        def pe_rows(n0, nk, lhs, done, first_bank=0):
            for k in range(nk):
                wp = piece(nc.tensor, n0 + k // 4)
                for t in range(T):
                    for h in range(2):
                        last = nc.tensor.matmul(bank(first_bank + 2 * t + h), lhs[:, k, 128 * t:128 * t + 128],
                                                wp[:, 1024 * (k % 4) + 512 * h:1024 * (k % 4) + 512 * h + 512],
                                                start=(k == 0), stop=(k == nk - 1))
                        if k == nk - 1:
                            last.then_inc(S(done), 1)
                if k % 4 == 3 and k < nk - 1:
                    last.then_inc(S(done.replace("done", "k")), 1)

        def split_columns(i, slot, hi, regions, norm=None):
            first = [len(regions) == 2 or j % 2 == 0 for j in range(len(regions))]
            wh, wl = three(hi, KC), three(slot, KC)
            xh, xl = XHI, XLO

            def one(o, cols, t, w, x, **flags):
                if t is None:
                    return nc.tensor.matmul(o, w[:, k, cols], x[:, k, :], **flags)
                return nc.tensor.matmul(o, x[:, k, 128 * t:128 * t + 128], w[:, k, cols], **flags)

            nc.tensor.wait_ge(S("hi_ready"), i + 1)
            for j, (o, cols, t) in enumerate(regions):
                for k in range(KC):
                    if norm is not None and j == 0 and k % 2 == 0:
                        nc.tensor.wait_ge(S("x_split"), 4 * (norm - 1) + k // 2 + 1)
                    one(o, cols, t, wh, xh, start=(k == 0 and first[j]), stop=False, skip_group_check=True)
                    last = one(o, cols, t, wh, xl, start=False, stop=False, skip_group_check=True)
            last.then_inc(S("hi_used"), 1)
            nc.tensor.wait_ge(S("lo_ready"), i + 1)
            lasts = []
            for o, cols, t in regions:
                for k in range(KC):
                    last = one(o, cols, t, wl, xh, start=False, stop=(k == KC - 1), skip_group_check=True)
                lasts.append(last)
            return lasts

        def conv_free(eng, g):
            if g < 6:
                eng.wait_ge(S("gconv_done"), g + 1)
            elif g < 9:
                eng.wait_ge(S("proj_act"), g - 5)
            elif g == 9:
                eng.wait_ge(*step("sc_prod"))
            else:
                eng.wait_ge(S("proj_act"), g - 6)

        @block.tensor
        def _(pe):
            mm = nc.tensor.matmul
            pe_norm(1)
            for j in range(PIN):
                regions = []
                for g in (2 * j, 2 * j + 1):
                    if g >= 4:
                        conv_free(pe, g - 4)
                    for c in range(2):
                        o = flat[:, 512 * (g % 4) + 256 * c:512 * (g % 4) + 256 * c + 256]
                        a0 = 256 * (g % 2)
                        if g < 13:
                            regions.append((o, slice(a0 + 128 * c, a0 + 128 * c + 128), None))
                        else:
                            regions.append((o, slice(a0, a0 + 256), c))
                lasts = split_columns(j, LO[j % NSLOT1], HI[j % 2], regions, norm=1 if j == 0 else None)
                lasts[1].then_inc(S("proj"), 1)
                lasts[3].then_inc(S("proj"), 1)
            pe.wait_ge(S("wab"), 2)
            wh, wl = (three(w, KC) for w in WAB)
            for t in range(T):
                o = flat[:, 2048 + 8 * t:2048 + 8 * t + 8]
                for k in range(KC):
                    xh, xl = (x[:, k, 128 * t:128 * t + 128] for x in (XHI, XLO))
                    mm(o, xh, wh[:, k, :], start=(k == 0), stop=False)
                    mm(o, xh, wl[:, k, :], start=False, stop=False)
                    last = mm(o, xl, wh[:, k, :], start=False, stop=(k == KC - 1))
            last.then_inc(*signal("ab_done"))

            scr = three(SCREP, KC)

            def ada(g, b, ks):
                wp = [three(piece(pe, FIRST["ada"] + 4 * g + j), KC) for j in range(4)]
                for k in ks:
                    for j in range(4):
                        last = mm(flat[32 * j:32 * j + 32, 512 * b:512 * b + 512], scr[:, k, :],
                                  wp[j][:, k, :], start=(k == 0), stop=(k == KC - 1))
                if k == KC - 1:
                    last.then_inc(S("ada"), 1)

            def pick(c):
                return ident[:, 32 * (c % 4):32 * (c % 4) + 1]

            def gate_rows(i):
                for h in range(2):
                    c = (4, 10)[i] + h
                    last = mm(bank(h), pick(c).broadcast_to([P, P]), three(MODR, 3)[:, c // 4, :], start=True, stop=True)
                last.then_inc(S("gtb"), 1)

            pe.wait_ge(*step("a8"))
            conv_free(pe, 11)
            mm(flat[:, 1536:1544], upto, A8, start=True, stop=True)
            mm(flat[:, 1544:1552], same, A8, start=True, stop=True).then_inc(*signal("gcol_done"))
            pe.wait_ge(S("abc"), 2)
            for m in range(M8):
                last = mm(flat[:, 2048 + 128 * m:2048 + 128 * m + 128], ABC[:, 128 * m:128 * m + 128], upto,
                          start=True, stop=True)
            last.then_inc(*signal("gb_done"))
            for m in range(M8):
                last = mm(flat[:, 3072 + 128 * m:3072 + 128 * m + 128], BBC[:, 128 * m:128 * m + 128], ident,
                          start=True, stop=True)
            last.then_inc(*signal("bb_done"))
            for i in range(2):
                pe.wait_ge(S("l2sq"), i + 1)
                if i == 0:
                    conv_free(pe, 12)
                    conv_free(pe, 13)
                else:
                    pe.wait_ge(S("gcol_in"), 1)
                for h in range(2):
                    last = mm(bank(2 * i + h), ones, (SQR if i == 0 else OT)[:, 512 * h:512 * h + 512], start=True, stop=True)
                last.then_inc(S("l2sum"), 1)
            pe.wait_ge(*step("screp"))
            pe.wait_ge(S("l2r"), 1)
            ada(0, 0, range(KC))
            pe.wait_ge(S("l2norm"), 2)
            pe.wait_ge(S("modr"), 1)
            for m in range(M8):
                t, h = divmod(m, NH)
                kt = KT[:, L * h + P * t:L * h + P * t + P]
                last = mm(flat[:, 128 * m:128 * m + 128], kt, kt, start=True, stop=True)
            last.then_inc(*signal("kk_done"))
            for m in range(M8):
                t, h = divmod(m, NH)
                last = mm(flat[:, 1024 + 128 * m:1024 + 128 * m + 128], KT[:, L * h + P * t:L * h + P * t + P],
                          QT[:, L * h + P * t:L * h + P * t + P], start=True, stop=True)
            last.then_inc(*signal("at_done"))
            pe.wait_ge(S("mlt"), 2)
            for m in range(M8):
                t, h = divmod(m, NH)
                last = nc.tensor.transpose(flat[:, 3072 + 128 * m:3072 + 128 * m + 128],
                                           KT[:, L * h + P * t:L * h + P * t + P], ident)
            last.then_inc(*signal("krow"))
            pe.wait_ge(*step("gdt"))
            for m in range(M8):
                t, h = divmod(m, NH)
                last = nc.tensor.transpose(flat[:, 2048 + 128 * m:2048 + 128 * m + 128],
                                           VT[:, L * h + P * t:L * h + P * t + P], ident)
            last.then_inc(*signal("vrow"))
            pe.wait_ge(S("krow_in"), 2)
            pe.wait_ge(S("vrow_in"), 1)
            pe.wait_ge(*step("atm"))
            for l in range(6):
                pe.wait_ge(S("cl"), l + 1)
                if l:
                    pe.wait_ge(S("xi"), 2 * l - 1)
                for m in range(M8):
                    s = slice(128 * m, 128 * m + 128)
                    last = mm(flat[:, s], CL[:, s], XI[:, s], start=True, stop=True)
                    if m % 4 == 3:
                        last.then_inc(S("y"), 1)
                pe.wait_ge(S("yl_act"), l + 1)
                pe.wait_ge(S("yl_dve"), l + 1)
                if l:
                    pe.wait_ge(S("xi"), 2 * l)
                for m in range(M8):
                    s = slice(128 * m, 128 * m + 128)
                    last = mm(flat[:, 1024 + 128 * m:1024 + 128 * m + 128], XIT[:, s], YL[:, s], start=True, stop=True)
                last.then_inc(S("xy"), 1)
                for m in range(M8):
                    s = slice(128 * m, 128 * m + 128)
                    last = mm(flat[:, 2048 + 128 * m:2048 + 128 * m + 128], YL[:, s], XIT[:, s], start=True, stop=True)
                last.then_inc(S("yx"), 1)
                if l in (1, 2):
                    ada(1, 7, range(4 * l - 4, 4 * l))
            pe.wait_ge(S("xi"), 12)
            for m in range(M8):
                s = slice(128 * m, 128 * m + 128)
                last = mm(flat[:, s], XIT[:, s], VB[:, s], start=True, stop=True)
            last.then_inc(*signal("u"))
            for m in range(M8):
                s = slice(128 * m, 128 * m + 128)
                last = mm(flat[:, 1024 + 128 * m:1024 + 128 * m + 128], KB[:, s], XIT[:, s], start=True, stop=True)
            last.then_inc(*signal("w"))
            ada(2, 6, range(KC))
            for n in range(NCH):
                t, b0 = n // 2, 64 * (n % 2)
                if n:
                    pe.wait_ge(S("state"), n)
                    pe.wait_ge(*step("wt_in"))
                    for h in range(NH):
                        m = NH * t + h
                        last = mm(flat[:, 2048 + 128 * h:2048 + 128 * h + 128], WT[:, 128 * m:128 * m + 128],
                                  ST[:, 128 * h:128 * h + 128], start=True, stop=True)
                    last.then_inc(S("ws"), 1)
                    if n > 1:
                        pe.wait_ge(S("os"), n - 1)
                    for h in range(NH):
                        m = NH * t + h
                        last = mm(flat[:, 2560 + 64 * h:2560 + 64 * h + 64], ST[:, 128 * h:128 * h + 128],
                                  QT[:, L * h + P * t + b0:L * h + P * t + b0 + 64], start=True, stop=True)
                    last.then_inc(S("qs"), 1)
                pe.wait_ge(S("vn"), n + 1)
                if n == 0:
                    pe.wait_ge(S("modr"), 3)
                if n < NCH - 1:
                    for h in range(NH):
                        m = NH * t + h
                        last = mm(flat[:, 3072 + 128 * h:3072 + 128 * h + 128], KD[b0:b0 + 64, 128 * m:128 * m + 128],
                                  VN[b0:b0 + 64, 128 * m:128 * m + 128], start=True, stop=True)
                    last.then_inc(S("kv"), 1)
                if n % 2:
                    if n > 1:
                        pe.wait_ge(S("ot"), 1)
                    for h in range(NH):
                        m = NH * t + h
                        last = mm(flat[:, 3584 + 128 * h:3584 + 128 * h + 128], VN[:, 128 * m:128 * m + 128],
                                  ATM[:, 128 * m:128 * m + 128], start=True, stop=True)
                    last.then_inc(S("av"), 1)
            pe.wait_ge(*step("osq"))
            pe.wait_ge(*step("wt_in"))
            for h in range(2):
                last = mm(bank(h), ones, XI[:, 512 * h:512 * h + 512], start=True, stop=True)
            last.then_inc(*signal("osum"))
            for hp in range(2):
                if hp:
                    pe.wait_ge(S("sb_lom"), 1)
                for i in range(2):
                    r = slice(64 * i, 64 * i + 64)
                    q = SBQ[r, L * hp:L * hp + L]
                    mm(flat[:, 1024 + 512 * i:1024 + 512 * i + 256], SBK[r, L * hp:L * hp + 128], q,
                       start=True, stop=True)
                    last = mm(flat[:, 1024 + 512 * i + 256:1024 + 512 * i + 384], SBK[r, L * hp + 128:L * hp + 256],
                              q[:, 128:256], start=True, stop=True)
                last.then_inc(S("sb_z"), 1)
                if hp == 0:
                    pe.wait_ge(S("ot"), 2)
                    modr = three(MODR, 3)
                    for i, c0 in enumerate((0, 2, 6, 8)):
                        for k in range(KC):
                            c = c0 + k // 4
                            last = mm(flat[:, 3584 + 8 * i + k:3584 + 8 * i + k + 1],
                                      modr[:, c // 4, 128 * (k % 4):128 * (k % 4) + 128], pick(c), start=True, stop=True)
                    last.then_inc(*signal("modc"))
                    pe.wait_ge(*step("orinv"))
                else:
                    pe.wait_ge(S("gtb_in"), 1)
                gate_rows(hp)
                pe.wait_ge(S("sb_lom"), hp + 1)
                if hp:
                    pe.wait_ge(S("sb_lb"), 1)
                for i in range(2):
                    o = 2048 + 512 * i
                    lom = SB1[:, 384 * i:384 * i + 384]
                    mm(flat[:, o:o + 256], after, lom[:, 0:256], start=True, stop=False)
                    mm(flat[:, o + 128:o + 256], ones, lom[:, 256:384], start=False, stop=True)
                    last = mm(flat[:, o + 256:o + 384], after, lom[:, 256:384], start=True, stop=True)
                last.then_inc(S("sb_tail"), 1)
                pe.wait_ge(S("sb_a"), hp + 1)
                for i in range(2):
                    h = 2 * hp + i
                    o = 3072 + 256 * hp
                    a = SB2[:, 384 * i:384 * i + 384]
                    mm(flat[64 * i:64 * i + 64, o:o + 256], SBV[:, 64 * h:64 * h + 64], a[:, 0:256],
                       start=True, stop=False)
                    last = mm(flat[64 * i:64 * i + 64, o + 128:o + 256], SBV[:, 256 + 64 * h:256 + 64 * h + 64],
                              a[:, 256:384], start=False, stop=True)
                last.then_inc(S("sb_o"), 1)
                pe.wait_ge(S("sb_y"), hp + 1)
            pe.wait_ge(S("gtb_in"), 2)
            pe.wait_ge(*step("y_sc"))
            pe.wait_ge(*step("y_gdn"))
            pe_rows(FIRST["mo"], KC, YT, "mo_done")
            pe_norm(2)

            def up(j, i, slot, hi, norm=None):
                o = 512 * (4 + 2 * (j % 2))
                regions = [(flat[:, o + 256 * c:o + 256 * c + 256], slice(128 * c, 128 * c + 128), None) for c in range(4)]
                split_columns(i, slot, hi, regions, norm)[-1].then_inc(S("up"), 1)

            i0 = SPLIT.index(FIRST["up"])
            for j in range(UPEEL):
                if j >= 2:
                    pe.wait_ge(S("fconv_done"), 2 * (j - 1))
                up(j, i0 + j, LO[(FIRST["up"] + j) % NSLOT1], HI[(i0 + j) % 2], norm=2 if j == 0 else None)
            with pe.Fori(0, (PUP - UPEEL) // NSLOT1) as i:
                for j in range(UPEEL, UPEEL + NSLOT1):
                    pe.wait_ge(S("fconv_done"), 8 * i + 2 * (j - 1))
                    up(j, NSLOT1 * i + i0 + j, LO[(FIRST["up"] + j) % NSLOT1], HI[(i0 + j) % 2])
            pe.wait_ge(S("gt"), PUP)
            gh, gl = three(GTHI, 22), three(GTLO, 22)
            for j in range(PDN):
                n = FIRST["dn"] + j
                i = SPLIT.index(n)
                wh, wl = HI[i % 2], LO[n % NSLOT1]
                ks = range(4 * j, min(4 * j + 4, 2 * PUP))
                pe.wait_ge(S("hi_ready"), i + 1)
                for k in ks:
                    for t in range(T):
                        for g in (gh, gl):
                            for h in range(2):
                                o = 1024 * (k % 4) + 512 * h
                                last = mm(bank(2 * t + h), g[:, k, 128 * t:128 * t + 128], wh[:, o:o + 512],
                                          start=(k == 0 and g is gh), stop=False)
                last.then_inc(S("hi_used"), 1)
                pe.wait_ge(S("lo_ready"), i + 1)
                for t in range(T):
                    for h in range(2):
                        for k in ks:
                            o = 1024 * (k % 4) + 512 * h
                            last = mm(bank(2 * t + h), gh[:, k, 128 * t:128 * t + 128], wl[:, o:o + 512],
                                      start=False, stop=(k == 2 * PUP - 1))
                        if j == PDN - 1:
                            last.then_inc(S("down_done"), 1)
                if j < PDN - 1:
                    last.then_inc(S("down_k"), 1)
            pe_norm(3)
            for j in range(PIN2):
                n = FIRST["in2"] + j
                i = SPLIT.index(n)
                regions = []
                for g in (2 * j, 2 * j + 1):
                    b, a0 = 4 + g % 4, 256 * (g % 2)
                    if g >= 4:
                        pe.wait_ge(S("proj2_in"), g - 3)
                    if g < 8:
                        regions += [(flat[:, 512 * b + 256 * c:512 * b + 256 * c + 256],
                                     slice(a0 + 128 * c, a0 + 128 * c + 128), None) for c in range(2)]
                    else:
                        regions.append((bank(b), slice(0, 512), g % 2))
                lasts = split_columns(i, LO[n % NSLOT1], HI[i % 2], regions, norm=3 if j == 0 else None)
                lasts[len(lasts) // 2 - 1].then_inc(S("proj2"), 1)
                lasts[-1].then_inc(S("proj2"), 1)
            pe.wait_ge(*step("lamp"))
            mm(flat[:, 0:2], ones[0:64, :], lam2[0:64, 0:2], start=True, stop=True).then_inc(*signal("lams"))
            pe.wait_ge(*step("nlam"))
            pe.wait_ge(S("proj2_in"), 12)

            def scores(u):
                q, k = (DQ, DK) if u < 8 else (NQ, NK)
                c, r = (u % 8) // 2, slice(64 * (u % 2), 64 * (u % 2) + 64)
                if u >= 2:
                    pe.wait_ge(S("sc_in"), u - 1)
                for t in range(T):
                    last = mm(flat[:, 512 * (u % 2) + 256 * t:512 * (u % 2) + 256 * t + 256],
                              q[r, L * c + P * t:L * c + P * t + P], k[r, L * c:L * c + L], start=True, stop=True)
                last.then_inc(S("scores"), 1)

            def turn(v):
                pe.wait_ge(S("pa"), v + 1)
                if v >= 2:
                    pe.wait_ge(S("pt"), v - 1)
                for kt in range(T):
                    for qt in range(T):
                        o = 1024 + 512 * (v % 2) + 256 * kt + 128 * qt
                        last = nc.tensor.transpose(flat[:, o:o + 128],
                                                   PA[v % 2][:, 256 * qt + 128 * kt:256 * qt + 128 * kt + 128], ident)
                last.then_inc(S("pat"), 1)

            def apply(v):
                pe.wait_ge(S("pt"), v + 1)
                if v < 4:
                    dst, vv = flat[:, 2048 + 256 * v:2048 + 256 * v + 256], [DV[:, 512 * kt + 128 * v:512 * kt + 128 * v + 128] for kt in range(T)]
                else:
                    n = v - 4
                    o = 3072 + 256 * (n // 2)
                    dst = flat[64 * (n % 2):64 * (n % 2) + 64, o:o + 256]
                    vv = [NV[:, 512 * kt + 64 * n:512 * kt + 64 * n + 64] for kt in range(T)]
                for kt in range(T):
                    last = mm(dst, vv[kt], PT[v % 2][:, 256 * kt:256 * kt + 256], start=(kt == 0), stop=(kt == T - 1))
                last.then_inc(S("ov"), 1)

            v = 0
            for u in range(16):
                scores(u)
                if (u < 8 and u >= 3 and u % 2) or u >= 9:
                    turn(v)
                    if v:
                        apply(v - 1)
                    v += 1
            while v < 12:
                turn(v)
                apply(v - 1)
                v += 1
            apply(11)
            pe.wait_ge(*step("dsq"))
            for h in range(2):
                last = mm(bank(h), ones, DSQ[:, 512 * h:512 * h + 512], start=True, stop=True)
            last.then_inc(*signal("dsum"))
            pe.wait_ge(*step("y_diff"))
            pe.wait_ge(*step("y_nat"))
            pe_rows(FIRST["out"], KC, YT, "out_done")
            pe_norm(4)
            hT_ready(pe, 4)
            wr = three(vec("router"), KC)
            for t in range(T):
                for k in range(KC):
                    last = mm(flat[:, 2048 + 32 * t:2048 + 32 * t + 32], HT[:, k, 128 * t:128 * t + 128], wr[:, k, :],
                              start=(k == 0), stop=(k == KC - 1))
            last.then_inc(*signal("lg"))
            for t in range(T):
                for k in range(KC):
                    last = nc.tensor.transpose(flat[:, 1024 * t + 128 * k:1024 * t + 128 * k + 128],
                                               HT[:, k, 128 * t:128 * t + 128], ident)
                last.then_inc(S("h2r"), 1)
            pe.wait_ge(*step("mask"))
            mm(flat[:, 2560:2592], before, MASK[:, 0, :], start=True, stop=True)
            mm(flat[:, 2592:2624], before, MASK[:, 1, :], start=True, stop=False)
            mm(flat[:, 2592:2624], ones, MASK[:, 0, :], start=False, stop=True)
            for t in range(T):
                last = mm(flat[0:32, 2624:2625], MASK[:, t, :], ones[:, 0:1], start=(t == 0), stop=(t == T - 1))
            last.then_inc(*signal("pos"))
            pe.wait_ge(*step("cnr"))
            mm(flat[0:32, 3072:3073], before[0:32, 0:32], CNR[0:32], start=True, stop=True)
            mm(flat[0:1, 3073:3105], CNR[0:32], before[0:32, 0:32], start=True, stop=True)
            mm(flat[0:1, 3105:3137], CNR[0:32], ident[0:32, 0:32], start=True, stop=True)
            mm(flat[0:1, 3137:3138], CNR[0:32], ones[0:32, 0:1], start=True, stop=True).then_inc(*signal("cum"))
            pe.wait_ge(S("gate"), 2)
            for i, a in enumerate((PM, GATE)):
                for t in range(T):
                    o = 3584 + 256 * i + 128 * t
                    last = nc.tensor.transpose(flat[0:32, o:o + 128], a[:, t, :], ident)
            last.then_inc(*signal("pmt"))
            pe.wait_ge(S("pmt_in"), 1)
            pe.wait_ge(S("oh"), 2)
            for t in range(T):
                o = 2048 + NPMAX * t
                mm(flat[:, o:o + NPMAX], PMT[0:32, 128 * t:128 * t + 128], OH[0:32], start=True, stop=False)
                mm(flat[:, o:o + NPMAX], ones[0:32, :], RM[0:32], start=False, stop=True)
            for t in range(T):
                o = 2048 + 128 + NPMAX * t
                last = mm(flat[:, o:o + NPMAX], GTT[0:32, 128 * t:128 * t + 128], OH[0:32], start=True, stop=True)
            last.then_inc(*signal("pp"))
            pe.wait_ge(S("h2r_in"), 2)
            pe.wait_ge(S("b_in"), 16)
            pe.wait_ge(S("b1_parts"), 7)
            for t in range(T):
                for h in range(2):
                    mm(bank(2 * t + h), GTT[0:32, 128 * t:128 * t + 128], B2[0:32, 512 * h:512 * h + 512],
                       start=True, stop=False, skip_group_check=True)

            def gather():
                for t in range(T):
                    for q in range(4):
                        last = mm(flat[32 * q:32 * q + 32, 3072:3328], SEL[:, t, :], H2R[:, t, 256 * q:256 * q + 256],
                                  start=(t == 0), stop=(t == T - 1))
                last.then_inc(S("g"), 1)

            def gather_transpose():
                for b in range(2):
                    last = nc.tensor.transpose(flat[:, 3584 + 128 * b:3584 + 128 * b + 128], GS[:, 128 * b:128 * b + 128], ident)
                last.then_inc(S("h"), 1)

            def scatter(quarters, signal, release=False):
                for t in range(T):
                    for q in quarters:
                        r = slice(32 * q, 32 * q + 32)
                        o = 1024 * t + 256 * q
                        last = mm(flat[:, o:o + 256], SGT[r, 128 * t:128 * t + 128], YS[r, :], start=False, stop=False,
                                  skip_group_check=True)
                        if release and t == 0 and q == quarters[0]:
                            last.then_inc(S("wused"), 1)
                last.then_inc(S(signal), 1)

            def up1(loaded, release):
                for kk in range(4):
                    wp = loaded(kk)
                    for b in range(2):
                        for q in range(4):
                            last = mm(flat[32 * q:32 * q + 32, 2048:2560], XG[:, b, 32 * kk:32 * kk + 32],
                                      wp[:, 2048 * b + 512 * q:2048 * b + 512 * q + 512],
                                      start=(kk == 0 and b == 0), stop=(kk == 3 and b == 1))
                        if kk == 0 and b == 0:
                            for q in range(4):
                                mm(flat[32 * q:32 * q + 32, 2048:2560], OHB[0:3 * NE, :], B1P[0:3 * NE, 512 * q:512 * q + 512],
                                   start=False, stop=False)
                    if release and kk < 3:
                        last.then_inc(S("wused"), 1)
                last.then_inc(S("w1"), 1)

            def down1(loaded, release):
                for c in range(KC):
                    if c % 4 == 0:
                        wp = loaded(4 + c // 4)
                    for q in range(4):
                        last = mm(flat[32 * q:32 * q + 32, 3072:3328],
                                  AT[:, 128 * (c % 2) + 32 * (c // 2):128 * (c % 2) + 32 * (c // 2) + 32],
                                  wp[:, 1024 * (c % 4) + 256 * q:1024 * (c % 4) + 256 * q + 256],
                                  start=(c == 0), stop=(c == KC - 1))
                    if release and c == 3:
                        last.then_inc(S("wused"), 1)
                last.then_inc(S("w2"), 1)
                if release:
                    mm(flat[0:1, 2560:2561], ones[0:1, 0:1], ones[0:1, 0:1], start=True, stop=True).then_inc(S("wused"), 1)

            def one_pass(p, loaded, release):
                pe.wait_ge(S("xg"), p + 1)
                pe.wait_ge(S("ohb"), p + 1)
                up1(loaded, release)
                pe.wait_ge(S("y_in"), p + 1)
                pe.wait_ge(S("sgt_in"), p + 1)
                scatter((0, 2), "scat_a", release)
                pe.wait_ge(S("sel"), p + 2)
                gather()
                pe.wait_ge(S("scat_a"), p + 1)
                scatter((1, 3), "scat")
                pe.wait_ge(S("sg"), p + 1)
                for t in range(T):
                    last = nc.tensor.transpose(flat[:, 3584 + 128 * t:3584 + 128 * t + 128], SG[:, t, :], ident)
                last.then_inc(S("sgtp"), 1)
                pe.wait_ge(S("act"), p + 1)
                for b in range(2):
                    last = nc.tensor.transpose(flat[:, 2560 + 128 * b:2560 + 128 * b + 128], HID[:, 128 * b:128 * b + 128], ident)
                last.then_inc(S("at"), 1)
                pe.wait_ge(S("g_in"), p + 2)
                pe.wait_ge(S("sgt_in"), p + 2)
                gather_transpose()
                pe.wait_ge(S("at_in"), p + 1)
                down1(loaded, release)

            pe.wait_ge(S("sel"), 1)
            pe.wait_ge(*step("cum_in"))
            gather()
            pe.wait_ge(S("g_in"), 1)
            pe.wait_ge(S("pmt_in"), 1)
            gather_transpose()
            def expert(i, j):
                def loaded(r):
                    n = 6 * j + r
                    s = n % NSLOT
                    pe.wait_ge(S(f"slot{s}_loaded"), 16 * (EPIECES // NSLOT) * i + 16 * (slot_base[s] + n // NSLOT + 1))
                    return slot_of(n)

                first = pe.value_load(passes[0:1, bass.ds(ESTEP * i + j, 1)], min_val=0, max_val=NPMAX - 1)
                more = pe.value_load(passes[0:1, bass.ds(ESTEP * i + j + NE, 1)], min_val=0, max_val=L // CAP - 1)
                with pe.If(more > 0):
                    with pe.Fori(0, more) as r:
                        one_pass(first + r, loaded, False)
                one_pass(first + more, loaded, True)

            with pe.Fori(0, NTURN) as i:
                for j in range(ESTEP):
                    expert(i, j)
            for j in range(NE - NTURN * ESTEP):
                expert(NTURN, j)
            n_passes = pe.value_load(passes[0:1, 64:65], min_val=NE, max_val=NPMAX - 1)
            pe.wait_ge(S("y_in"), n_passes + 1)
            pe.wait_ge(S("sgt_in"), n_passes + 1)
            scatter((0, 2), "scat_a")
            pe.wait_ge(S("scat_a"), n_passes + 1)
            scatter((1, 3), "scat")

        @block.gpsimd
        def _(g):
            for i, n in enumerate(SPLIT):
                slot = ring[:, n % NSLOT1, :]
                g.wait_ge(S("hi_ready"), i + 1)
                g.tensor_tensor(LO[n % NSLOT1], slot, HI[i % 2].bitcast(F32), ALU.subtract).then_inc(S("lo_ready"), 1)
            nb = NB.rearrange("p (r w) -> p r w", w=64)
            g.wait_ge(S("const_in"), 16)
            g.wait_ge(S("natb_in"), 16)
            g.tensor_tensor(nb, nb, const("window").unsqueeze(1).broadcast_to([P, 64, 64]), ALU.add).then_inc(S("window"), 1)
            g.wait_ge(S("b1_in"), 48)
            done = 0

            def part(out, a, b=None):
                nonlocal done
                if b is None:
                    g.tensor_copy(out, a).then_inc(S("b1_parts"), 1)
                else:
                    g.tensor_tensor(out, a, b, ALU.subtract).then_inc(S("b1_parts"), 1)
                done += 1
                g.wait_ge(S("b1_parts"), done)

            blocks = [slice(NE * i, NE * i + NE) for i in range(3)]
            part(B1P[0:3 * NE, :], B1[0:3 * NE, :])
            for i in (1, 2):
                for r in blocks[i:]:
                    part(B1[r, :], B1[r, :], B1P[r, :])
                    part(B1P[r, :], B1[r, :])

        def linked(eng, name):
            n = [0]

            def link(ins):
                n[0] += 1
                ins.then_inc(S(name), 1)
                eng.wait_ge(S(name), n[0])
            return link

        def act_square(i):
            a = nc.scalar
            if i == 1:
                a.wait_ge(S("x_in"), 16)
            else:
                a.wait_ge(S(f"x{i}"), T)
            for t in range(T):
                a.activation(XN[:, t, :], X[:, t, :], ACT.Square, accum_out=ssq[:, t:t + 1]).then_inc(S("ssq"), 1)

        def act_norm(i, scale, shift=None):
            a = nc.scalar
            act_square(i)
            a.wait_ge(S("rinv"), NORMS.index(i) + 1)
            a.activation(rstd, mean, ACT.Sqrt).then_inc(S("rstd"), 1)
            a.wait_ge(S("vec_in"), 16)
            for b in (1, 3):
                a.wait_ge(S("xT"), 4 * (i - 1) + b + 1)
                for k in (2 * b, 2 * b + 1):
                    sh = 0.0 if shift is None else shift[:, k:k + 1]
                    last = a.activation(HT[:, k, :], flat[:, 256 * k:256 * k + 256], ACT.Identity,
                                        bias=sh, scale=scale[:, k:k + 1])
                last.then_inc(S("hT_act"), 1)

        def high(out, x):
            return nc.vector.tensor_copy(out, x)

        def split_hi(i):
            v, n = nc.vector, SPLIT[i]
            slot = piece(v, n)
            if i >= 2:
                v.wait_ge(S("hi_used"), i - 1)
                v.wait_ge(S("lo_ready"), i - 1)
            high(HI[i % 2], slot).then_inc(S("hi_ready"), 1)

        def split_x(link, norm):
            v = nc.vector
            for b in range(4):
                if b % 2:
                    v.wait_ge(S("hT_act"), 2 * (norm - 1) + b // 2 + 1)
                else:
                    v.wait_ge(S("hT_dve"), 2 * (norm - 1) + b // 2 + 1)
                x, hi = HT[:, 2 * b:2 * b + 2, :], XHI[:, 2 * b:2 * b + 2, :]
                link(high(hi, x))
                v.tensor_tensor(XLO[:, 2 * b:2 * b + 2, :], x, hi.bitcast(F32), ALU.subtract).then_inc(S("x_split"), 1)

        def dve_norm(link, i, scale, shift=None, meanwhile=()):
            v = nc.vector
            v.wait_ge(S("ssq"), SQUARES[i])
            link(v.tensor_scalar(mean, ssq[:, 0:2], 1.0 / D, EPS, ALU.mult, ALU.add))
            v.reciprocal(mean, mean).then_inc(S("rinv"), 1)
            v.wait_ge(S("rstd"), NORMS.index(i) + 1)
            for t in range(T):
                v.tensor_scalar(XN[:, t, :], X[:, t, :], rstd[:, t:t + 1], None, ALU.mult).then_inc(S("xn"), 1)
            for j in meanwhile:
                split_hi(j)
            v.wait_ge(S("vec_in"), 16)
            for b in (0, 2):
                v.wait_ge(S("xT"), 4 * (i - 1) + b + 1)
                for k in (2 * b, 2 * b + 1):
                    if shift is None:
                        last = v.tensor_scalar(HT[:, k, :], flat[:, 256 * k:256 * k + 256], scale[:, k:k + 1], None, ALU.mult)
                    else:
                        last = v.tensor_scalar(HT[:, k, :], flat[:, 256 * k:256 * k + 256], scale[:, k:k + 1],
                                               shift[:, k:k + 1], ALU.mult, ALU.add)
                last.then_inc(S("hT_dve"), 1)

        @block.scalar
        def _(a):
            link = linked(a, "act_chain")
            f = a.activation
            act_norm(1, vec("norm_mix"))
            gconv = three(vec("gconv"), 12)
            for j in range(3):
                dst = (KT, QT, VT)[j]
                for pp in range(2):
                    g = 2 * j + pp
                    a.wait_ge(S("proj"), g + 1)
                    for c in range(2):
                        ch = 2 * pp + c
                        last = f(dst[:, L * ch:L * ch + L], flat[:, 512 * (g % 4) + 256 * c:512 * (g % 4) + 256 * c + 256],
                                 ACT.Copy, scale=gconv[:, 4 * j + ch, 3:4])
                    last.then_inc(S("gconv_first"), 1)
            for g in (6, 7):
                a.wait_ge(S("proj"), g + 1)
                f(GZ[:, 512 * (g - 6):512 * (g - 6) + 512], bank(g % 4), ACT.Silu).then_inc(S("proj_act"), 1)
            for j in range(3):
                dst = (KT, QT, VT)[j]
                a.wait_ge(S("gconv_done"), 2 * j + 2)
                f(dst, dst, ACT.Silu).then_inc(S("gsilu"), 1)
            a.wait_ge(S("proj"), 9)
            f(SCP, bank(0), ACT.Copy).then_inc(S("proj_act"), 1)
            a.wait_ge(S("proj"), 11)
            f(SCB, bank(2), ACT.Copy).then_inc(S("proj_act"), 1)
            a.wait_ge(S("proj"), 12)
            f(SBQ, bank(3), ACT.Copy, scale=0.125).then_inc(S("proj_act"), 1)
            a.wait_ge(S("proj"), 13)
            f(SBK, bank(0), ACT.Copy).then_inc(S("proj_act"), 1)
            a.wait_ge(S("proj"), 14)
            f(SBV, bank(1), ACT.Copy).then_inc(S("proj_act"), 1)
            link(f(silc, vec("c"), ACT.Silu))
            a.wait_ge(S("gu"), 3)
            link(f(v8, v8, ACT.Exp, scale=-1.0))
            f(v8, v8, ACT.Ln, bias=1.0).then_inc(S("gl"), 1)
            f(ea4, vec("alog"), ACT.Exp).then_inc(S("gl"), 1)
            f(e8, e8, ACT.Exp, scale=-1.0).then_inc(S("gl"), 1)
            a.wait_ge(S("gsilu"), 2)
            f(SQR, KT, ACT.Square).then_inc(S("l2sq"), 1)
            f(OT, QT, ACT.Square).then_inc(S("l2sq"), 1)
            a.wait_ge(S("l2r"), 1)
            f(SQR, SQR, ACT.Sqrt).then_inc(S("l2s"), 1)
            a.wait_ge(S("l2r"), 2)
            f(OT, OT, ACT.Sqrt, scale=1.0 / P).then_inc(S("l2s"), 1)
            a.wait_ge(S("gcol_in"), 1)
            f(EGC, GCOL, ACT.Exp).then_inc(S("egc"), 1)
            a.wait_ge(*step("egl_d"))
            f(EGL, EGL, ACT.Exp).then_inc(S("egc"), 1)
            a.wait_ge(*step("gb_done"))
            f(EG, bank(4, 2), ACT.Exp).then_inc(*signal("eg"))
            a.wait_ge(*step("gdt"))
            f(DT, DT, ACT.Exp).then_inc(*signal("dt"))
            a.wait_ge(*step("krow"))
            for m in range(M8):
                last = f(KD[:, 128 * m:128 * m + 128], flat[:, 3072 + 128 * m:3072 + 128 * m + 128], ACT.Copy,
                         scale=EGL[:, m:m + 1])
            last.then_inc(S("krow_in"), 1)
            for l in range(6):
                a.wait_ge(S("y"), 2 * l + 1)
                if l:
                    a.wait_ge(S("yx"), l)
                f(YL[:, 0:512], bank(0), ACT.Copy).then_inc(S("yl_act"), 1)
            a.wait_ge(*step("w"))
            f(WT, bank(2, 2), ACT.Copy).then_inc(*signal("wt_in"))
            for n in range(1, NCH):
                a.wait_ge(S("qs"), n)
                o3 = OS.rearrange("p (h c) -> p h c", h=NH)[:, :, 64 * n:64 * n + 64]
                f(o3, flat[:, 2560:2816].rearrange("p (h c) -> p h c", h=NH), ACT.Copy).then_inc(S("os"), 1)
            a.wait_ge(S("ot"), 2)
            f(XI, OT, ACT.Square).then_inc(*signal("osq"))
            a.wait_ge(*step("orinv"))
            f(XI, XI, ACT.Sqrt).then_inc(*signal("orstd"))
            for hp in range(2):
                a.wait_ge(S("sb_z"), hp + 1)
                if hp:
                    a.wait_ge(S("sb_o"), 1)
                z3 = flat[:, 1024:2048].rearrange("p (i c) -> p i c", i=2)[:, :, 0:384]
                link(f(three(SB1, 2), z3, ACT.Abs))
                link(f(SB1, SB1, ACT.Exp, scale=-1.0))
                f(SB1, SB1, ACT.Ln, bias=1.0).then_inc(S("sb_ln"), 1)
                a.wait_ge(S("sb_lb"), hp + 1)
                f(SB2, SB2, ACT.Exp).then_inc(S("sb_exp"), 1)
                a.wait_ge(S("sb_o"), hp + 1)
                f(YT[:, 6 + hp, :], flat[:, 3072 + 256 * hp:3072 + 256 * hp + 256], ACT.Copy).then_inc(S("sb_y"), 1)
            a.wait_ge(S("sb_y"), 2)
            a.wait_ge(S("gtb_in"), 2)
            act_norm(2, vec("norm_ffn"))
            fc3 = three(vec("fconv"), PUP)

            for j in range(PUP):
                a.wait_ge(S("up"), j + 1)
                o = 2048 + 1024 * (j % 2)
                uc = (UC, UC2)[j % 2]
                if j >= 2:
                    a.wait_ge(S("gt"), j - 1)
                for c in range(4):
                    last = f(uc[:, 256 * c:256 * c + 256], flat[:, o + 256 * c:o + 256 * c + 256], ACT.Copy,
                             scale=fc3[:, j, 3 * c + 2:3 * c + 3])
                last.then_inc(S("fconv_first"), 1)
                a.wait_ge(S("fconv_done"), 2 * j + 2)
                f(uc[:, 0:512], uc[:, 0:512], ACT.Silu).then_inc(S("usilu"), 1)
            a.wait_ge(S("xf"), T)
            for t in range(T):
                f(XN[:, t, :], X[:, t, :], ACT.Square, accum_out=ssq[:, t:t + 1]).then_inc(S("ssq"), 1)
            a.wait_ge(S("rinv"), NORMS.index("f") + 1)
            f(rstd, mean, ACT.Sqrt).then_inc(S("rstd"), 1)
            act_norm(3, GW1, MODC[:, 0:8])
            for g in range(12):
                a.wait_ge(S("proj2"), g + 1)
                dst = (DQ, DK, NQ, NK, DV, NV)[g // 2][:, 512 * (g % 2):512 * (g % 2) + 512]
                f(dst, bank(4 + g % 4), ACT.Copy, scale=0.125 if g // 2 in (0, 2) else 1.0).then_inc(S("proj2_in"), 1)
            a.wait_ge(*step("lams"))
            f(lam2[:, 2:4], flat[:, 0:2], ACT.Exp).then_inc(*signal("elam"))

            def probs(u):
                s = three(SC[u % 2], T)
                a.wait_ge(S("nmax"), u + 1)
                for t in range(T):
                    last = f(s[:, t, :], s[:, t, :], ACT.Exp, bias=nmx[:, 2 * (u % 2) + t:2 * (u % 2) + t + 1],
                             accum_out=sme[:, 2 * (u % 2) + t:2 * (u % 2) + t + 1])
                    last.then_inc(S("probs"), 1)

            def evac(v):
                a.wait_ge(S("pat"), v + 1)
                if v >= 2:
                    a.wait_ge(S("ov"), v - 1)
                f(PT[v % 2], bank(2 + v % 2), ACT.Copy).then_inc(S("pt"), 1)

            v = 0
            for u in range(16):
                if (u < 8 and u >= 3 and u % 2) or u >= 9:
                    evac(v)
                    v += 1
                probs(u)
            while v < 12:
                evac(v)
                v += 1
            a.wait_ge(S("ov"), 12)
            f(DSQ, bank(4, 2), ACT.Square).then_inc(*signal("dsq"))
            f(DO, bank(4, 2), ACT.Copy).then_inc(*signal("do"))
            f(YT[:, 4:8, :], three(bank(6, 2), 4), ACT.Copy).then_inc(*signal("y_nat"))
            a.wait_ge(*step("drinv"))
            f(DRS, DRS, ACT.Sqrt).then_inc(*signal("drstd"))
            a.wait_ge(S("out_done"), 4)
            for t in range(T):
                for h in range(2):
                    f(XN[:, t, 512 * h:512 * h + 512], bank(2 * t + h), ACT.Square,
                      accum_out=ssq[:, 2 * t + h:2 * t + h + 1]).then_inc(S("ssq"), 1)
            a.wait_ge(S("rinv"), NORMS.index("m") + 1)
            f(rstd, mean, ACT.Sqrt).then_inc(S("rstd"), 1)
            act_norm(4, GW2, MODC[:, 16:24])
            a.wait_ge(*step("lgs"))
            f(EE, EE, ACT.Exp).then_inc(*signal("ee"))
            a.wait_ge(S("h2r"), 2)
            f(H2R[:, 1, :], bank(2, 2), ACT.Copy).then_inc(S("h2r_in"), 1)
            a.wait_ge(S("h"), 1)
            f(XG.rearrange("p a b -> p (a b)"), flat[:, 3584:3840], ACT.Copy).then_inc(S("xg"), 1)
            a.wait_ge(*step("cum_in"))
            n_passes = a.value_load(passes[0:1, 64:65], min_val=NE, max_val=NPMAX - 1)
            with a.Fori(0, n_passes) as p:
                a.wait_ge(S("glu"), p + 1)
                f(SIG, GLU, ACT.Sigmoid, scale=1.702).then_inc(S("sig"), 1)
                a.wait_ge(S("sgtp"), p + 1)
                a.wait_ge(S("scat"), p + 1)
                f(SGT, flat[:, 3584:3840], ACT.Copy).then_inc(S("sgt_in"), 1)
                a.wait_ge(S("at"), p + 1)
                f(AT, flat[:, 2560:2816], ACT.Copy).then_inc(S("at_in"), 1)
                a.wait_ge(S("h"), p + 2)
                f(XG.rearrange("p a b -> p (a b)"), flat[:, 3584:3840], ACT.Copy).then_inc(S("xg"), 1)
                a.wait_ge(S("w2"), p + 1)
                f(YS, flat[:, 3072:3328], ACT.Copy).then_inc(S("y_in"), 1)
            a.wait_ge(S("scat"), n_passes + 1)
            for t in range(T):
                for h in range(2):
                    f(XN[:, t, 512 * h:512 * h + 512], bank(2 * t + h), ACT.Square,
                      accum_out=ssq[:, 2 * t + h:2 * t + h + 1]).then_inc(S("ssq"), 1)
            a.wait_ge(S("rinv"), NORMS.index("e") + 1)
            f(rstd, mean, ACT.Sqrt).then_inc(S("rstd"), 1)

        @block.vector
        def _(v):
            link = linked(v, "dve_chain")
            tt, ts, stt = v.tensor_tensor, v.tensor_scalar, v.scalar_tensor_tensor
            v.wait_ge(S("vec_in"), 16)
            link(high(WAB[0], vec("ab")))
            tt(WAB[1], vec("ab"), WAB[0].bitcast(F32), ALU.subtract).then_inc(S("wab"), 2)
            dve_norm(link, 1, vec("norm_mix"), meanwhile=(0,))
            split_x(link, 1)
            split_hi(1)
            gconv = three(vec("gconv"), 12)
            for j in range(3):
                dst = (KT, QT, VT)[j]
                split_hi(j + 2)
                for pp in range(2):
                    g = 2 * j + pp
                    v.wait_ge(S("gconv_first"), g + 1)
                    for tap in (2, 1, 0):
                        sh = 3 - tap
                        for c in range(2):
                            ch = 2 * pp + c
                            o = 512 * (g % 4) + 256 * c
                            d = dst[:, L * ch + sh:L * ch + L]
                            last = stt(d, flat[:, o:o + 256 - sh], gconv[:, 4 * j + ch, tap:tap + 1], d, ALU.mult, ALU.add)
                            if tap:
                                link(last)
                    last.then_inc(S("gconv_done"), 1)
                    v.wait_ge(S("gconv_done"), g + 1)
            split_hi(5)
            split_hi(6)
            v.wait_ge(S("proj"), 10)
            v.wait_ge(S("proj_act"), 3)
            tt(SCP, bank(1), SCP, ALU.mult).then_inc(*signal("sc_prod"))
            ab = flat[:, 2048:2064].rearrange("p (t c) -> p t c", t=T)
            v.wait_ge(*step("ab_done"))
            link(tt(three(u8, T), ab[:, :, 0:4], vec("dtb").unsqueeze(1).broadcast_to([P, T, 4]), ALU.add))
            link(v.tensor_copy(three(e8, T), ab[:, :, 4:8]))
            link(stt(v8, u8, -1.0, u8, ALU.mult, ALU.max))
            ts(u8, u8, 0.0, None, ALU.max).then_inc(S("gu"), 3)
            v.wait_ge(S("gl"), 3)
            link(tt(u8, u8, v8, ALU.add))
            stt(three(A8, T), three(u8, T), -1.0, ea4.unsqueeze(1).broadcast_to([P, T, 4]), ALU.mult, ALU.mult).then_inc(*signal("a8"))
            link(ts(e8, e8, 1.0, None, ALU.add))
            link(v.reciprocal(BET, e8))
            v.wait_ge(*step("a8"))
            v.tensor_copy(three(ABC, M8), A8.unsqueeze(2).broadcast_to([P, M8, P])).then_inc(S("abc"), 1)
            v.tensor_copy(three(BBC, M8), BET.unsqueeze(2).broadcast_to([P, M8, P])).then_inc(S("abc"), 1)
            v.wait_ge(S("act_chain"), 1)
            v.wait_ge(S("proj"), 14)
            v.tensor_copy(three(SCREP, KC), silc.unsqueeze(2).broadcast_to([P, KC, 32])).then_inc(*signal("screp"))
            modr = three(MODR, 3)

            def modulation(g, b):
                v.wait_ge(S("bada_in"), 16)
                v.wait_ge(S("ada"), g + 1)
                tt(modr[:, g, :], modr[:, g, :], bank(b), ALU.add).then_inc(S("modr"), 1)

            for i in range(2):
                r = (SQR, OT)[i]
                v.wait_ge(S("l2sum"), i + 1)
                link(ts(r, bank(2 * i, 2), EPS, None, ALU.add))
                v.reciprocal(r, r).then_inc(S("l2r"), 1)
                if i == 0:
                    v.wait_ge(*step("gcol_done"))
                    v.tensor_copy(GCOL, flat[:, 1536:1544])
                    v.tensor_copy(GLAST, flat[:, 1544:1552]).then_inc(S("gcol_in"), 1)
                    v.wait_ge(S("gcol_in"), 1)
                    tt(EGL, GLAST, GCOL, ALU.subtract).then_inc(*signal("egl_d"))
            for i in range(2):
                v.wait_ge(S("l2s"), i + 1)
                d = (KT, QT)[i]
                tt(d, d, (SQR, OT)[i], ALU.mult).then_inc(S("l2norm"), 1)
            modulation(0, 0)
            v.wait_ge(S("egc"), 1)
            link(tt(BEG, BET, EGC, ALU.mult))
            v.wait_ge(*step("eg"))
            v.wait_ge(S("l2norm"), 2)
            for m in range(M8):
                last = ts(DT[:, 128 * m:128 * m + 128], flat[:, 2048 + 128 * m:2048 + 128 * m + 128],
                          GCOL[:, m:m + 1], 0.0, ALU.subtract, ALU.min)
            last.then_inc(*signal("gdt"))
            v.wait_ge(*step("dt"))
            v.wait_ge(*step("kk_done"))
            tt(MLT, bank(0, 2), DT, ALU.mult).then_inc(S("mlt"), 1)
            v.wait_ge(*step("bb_done"))
            v.wait_ge(S("mlt"), 1)
            tt(MLT, MLT, bank(6, 2), ALU.mult).then_inc(S("mlt"), 1)
            v.wait_ge(*step("at_done"))
            link(tt(ATM, bank(2, 2), DT, ALU.mult))
            tt(three(ATM, M8), three(ATM, M8), upto.unsqueeze(1).broadcast_to([P, M8, P]), ALU.mult).then_inc(*signal("atm"))
            qv, ev = QT.rearrange("p (h t c) -> p h t c", h=NH, t=T), EG.rearrange("p (t h c) -> p h t c", h=NH, t=T)
            for h in range(NH):
                last = tt(qv[:, h], qv[:, h], ev[:, h], ALU.mult)
            v.wait_ge(S("krow_in"), 1)
            for m in range(M8):
                last = ts(KB[:, 128 * m:128 * m + 128], flat[:, 3072 + 128 * m:3072 + 128 * m + 128],
                          BEG[:, m:m + 1], None, ALU.mult)
            last.then_inc(S("krow_in"), 1)
            v.wait_ge(*step("vrow"))
            for m in range(M8):
                last = ts(VB[:, 128 * m:128 * m + 128], flat[:, 2048 + 128 * m:2048 + 128 * m + 128],
                          BET[:, m:m + 1], None, ALU.mult)
            last.then_inc(S("vrow_in"), 1)
            v.tensor_copy(three(XI, M8), ident.unsqueeze(1).broadcast_to([P, M8, P]))
            link(v.tensor_copy(three(XIT, M8), ident.unsqueeze(1).broadcast_to([P, M8, P])))
            v.wait_ge(S("mlt"), 2)
            def cross(l):
                tt(three(CL, M8), three(MLT, M8), level[:, l, :].unsqueeze(1).broadcast_to([P, M8, P]), ALU.mult).then_inc(S("cl"), 1)

            cross(0)
            for l in range(6):
                v.wait_ge(S("y"), 2 * l + 2)
                v.tensor_copy(YL[:, 512:1024], bank(1)).then_inc(S("yl_dve"), 1)
                if l < 5:
                    cross(l + 1)
                v.wait_ge(S("xy"), l + 1)
                tt(XI, XI, bank(2, 2), ALU.add).then_inc(S("xi"), 1)
                v.wait_ge(S("yx"), l + 1)
                tt(XIT, XIT, bank(4, 2), ALU.add).then_inc(S("xi"), 1)
                v.wait_ge(S("xi"), 2 * l + 2)
                if l == 3:
                    modulation(1, 7)
            v.wait_ge(*step("u"))
            link(v.tensor_copy(U, bank(0, 2)))
            eg4 = EG.rearrange("p (m c) -> p m c", m=M8)
            sc3, sp3, sy3, sb3 = (three(z, 2) for z in (vec("sconv"), SCP, SCY, SCB))
            v.wait_ge(*step("sc_prod"))
            for tap in (2, 1, 0):
                sh = 2 - tap
                for c in range(2):
                    w = sc3[:, c, tap:tap + 1]
                    if tap == 2:
                        link(ts(sy3[:, c, :], sp3[:, c, :], w, None, ALU.mult))
                    else:
                        link(stt(sy3[:, c, sh:L], sp3[:, c, 0:L - sh], w, sy3[:, c, sh:L], ALU.mult, ALU.add))
            v.wait_ge(S("proj_act"), 4)
            tt(YT[:, 0:2, :], sy3, sb3, ALU.mult).then_inc(*signal("y_sc"))
            modulation(2, 6)
            link(v.memset(OS.rearrange("p (h c) -> p h c", h=NH)[:, :, 0:64], 0.0))
            for n in range(NCH):
                t, b0 = n // 2, 64 * (n % 2)
                cols = slice(512 * t, 512 * t + 512)
                rows_ = slice(b0, b0 + 64)
                if n == 0:
                    v.tensor_copy(VN[rows_, cols], U[rows_, cols]).then_inc(S("vn"), 1)
                else:
                    v.wait_ge(S("ws"), n)
                    stt(VN[rows_, cols], flat[rows_, 2048:2560], -1.0, U[rows_, cols], ALU.mult, ALU.add).then_inc(S("vn"), 1)
                if n < NCH - 1:
                    v.wait_ge(S("kv"), n + 1)
                    if n:
                        v.wait_ge(S("qs"), n)
                    if n == 0:
                        v.tensor_copy(ST, bank(6)).then_inc(S("state"), 1)
                    else:
                        v.wait_ge(S("state"), n)
                        for h in range(NH):
                            s = slice(128 * h, 128 * h + 128)
                            last = stt(ST[:, s], ST[:, s], eg4[:, NH * t + h, b0 + 63:b0 + 64], flat[:, 3072 + 128 * h:3072 + 128 * h + 128],
                                       ALU.mult, ALU.add)
                        last.then_inc(S("state"), 1)
                if n % 2:
                    v.wait_ge(S("av"), t + 1)
                    v.wait_ge(S("os"), n)
                    dst = OT.rearrange("p (h c) -> p h c", h=NH)[:, :, 128 * t:128 * t + 128]
                    tt(dst, three(bank(7), NH), OS.rearrange("p (h c) -> p h c", h=NH)[:, :, 128 * t:128 * t + 128],
                       ALU.add).then_inc(S("ot"), 1)
            v.wait_ge(*step("osum"))
            link(ts(XI, bank(0, 2), 1.0 / P, EPS, ALU.mult, ALU.add))
            v.reciprocal(XI, XI).then_inc(*signal("orinv"))
            v.wait_ge(S("proj_act"), 2)
            v.wait_ge(S("ot"), 2)
            link(stt(OT, OT, vec("gnorm"), GZ, ALU.mult, ALU.mult))
            v.wait_ge(*step("orstd"))
            tt(YT[:, 2:6, :], three(OT, NH), three(XI, NH), ALU.mult).then_inc(*signal("y_gdn"))
            z3 = flat[:, 1024:2048].rearrange("p (i c) -> p i c", i=2)[:, :, 0:384]
            tail3 = flat[:, 2048:3072].rearrange("p (i c) -> p i c", i=2)[:, :, 0:384]
            s1, s2 = three(SB1, 2), three(SB2, 2)
            mask = before.unsqueeze(1).broadcast_to([P, 2, P])
            for hp in range(2):
                v.wait_ge(S("sb_ln"), hp + 1)
                link(stt(s2, z3, 0.0, s1, ALU.min, ALU.subtract))
                link(stt(s1, z3, -1.0, s2, ALU.mult, ALU.add))
                tt(s1[:, :, 0:128], s1[:, :, 0:128], mask, ALU.mult)
                tt(s1[:, :, 256:384], s1[:, :, 256:384], mask, ALU.mult).then_inc(S("sb_lom"), 1)
                v.wait_ge(S("sb_tail"), hp + 1)
                tt(s2, s2, tail3, ALU.add).then_inc(S("sb_lb"), 1)
                v.wait_ge(S("sb_exp"), hp + 1)
                tt(s2[:, :, 0:128], s2[:, :, 0:128], mask, ALU.mult)
                tt(s2[:, :, 256:384], s2[:, :, 256:384], mask, ALU.mult).then_inc(S("sb_a"), 1)
                if hp == 0:
                    v.wait_ge(*step("modc"))
                    link(v.tensor_copy(MODC, flat[:, 3584:3616]))
                    link(stt(GW1, MODC[:, 8:16], 1.0, vec("pre_mix"), ALU.add, ALU.mult))
                    link(stt(GW2, MODC[:, 24:32], 1.0, vec("pre_ffn"), ALU.add, ALU.mult))
                    v.wait_ge(S("rows_in"), 16)
                v.wait_ge(S("gtb"), hp + 1)
                g = (G1B, G2B)[hp]
                tt(g, g, bank(0, 2), ALU.mult).then_inc(S("gtb_in"), 1)

            def residual(done, signal, n):
                for t in range(T):
                    for h in range(2):
                        v.wait_ge(S(done), 2 * t + h + 1)
                        last = tt(X[:, t, 512 * h:512 * h + 512], X[:, t, 512 * h:512 * h + 512], bank(2 * t + h), ALU.add)
                    last.then_inc(S(signal), 1)

            residual("mo_done", "x2", 1)
            i_up = SPLIT.index(FIRST["up"])
            dve_norm(link, 2, vec("norm_ffn"), meanwhile=(i_up,))
            split_x(link, 2)
            split_hi(i_up + 1)
            fc3 = three(vec("fconv"), PUP)
            for j in range(PUP):
                uc = (UC, UC2)[j % 2]
                split_hi(i_up + j + 2)
                v.wait_ge(S("fconv_first"), j + 1)
                o = 2048 + 1024 * (j % 2)
                for tap in (1, 0):
                    sh = 2 - tap
                    for c in range(4):
                        last = stt(uc[:, 256 * c + sh:256 * c + 256], flat[:, o + 256 * c:o + 256 * c + 256 - sh],
                                   fc3[:, j, 3 * c + tap:3 * c + tap + 1], uc[:, 256 * c + sh:256 * c + 256], ALU.mult, ALU.add)
                    last.then_inc(S("fconv_done"), 1)
                    v.wait_ge(S("fconv_done"), 2 * j + 2 - tap)
                v.wait_ge(S("usilu"), j + 1)
                link(tt(uc[:, 0:512], uc[:, 0:512], uc[:, 512:1024], ALU.mult))
                link(high(GTHI[:, 512 * j:512 * j + 512], uc[:, 0:512]))
                tt(GTLO[:, 512 * j:512 * j + 512], uc[:, 0:512], GTHI[:, 512 * j:512 * j + 512].bitcast(F32), ALU.subtract).then_inc(S("gt"), 1)
            for j in range(2, PDN + 1):
                split_hi(SPLIT.index(FIRST["dn"]) + j)
            residual("down_done", "xf", 2)
            v.wait_ge(S("ssq"), SQUARES["f"])
            link(ts(mean, ssq[:, 0:2], 1.0 / D, EPS, ALU.mult, ALU.add))
            v.reciprocal(mean, mean).then_inc(S("rinv"), 1)
            v.wait_ge(S("rstd"), NORMS.index("f") + 1)
            for t in range(T):
                stt(X[:, t, :], X[:, t, :], rstd[:, t:t + 1], WFIN, ALU.mult, ALU.mult).then_inc(S("x3"), 1)
            v.wait_ge(S("x3"), T)
            i_in2 = SPLIT.index(FIRST["in2"])
            dve_norm(link, 3, GW1, MODC[:, 0:8], meanwhile=(i_in2 + 1,))
            split_x(link, 3)
            for j in range(2, PIN2):
                split_hi(i_in2 + j)
            lam = vec("lam")
            tt(lam2[0:64, 0:2], lam[0:64, 0:2], lam[0:64, 2:4], ALU.mult).then_inc(*signal("lamp"))
            v.wait_ge(*step("elam"))
            link(tt(nlam, lam2[:, 3:4], lam2[:, 2:3], ALU.subtract))
            ts(nlam, nlam, -0.2, None, ALU.add).then_inc(*signal("nlam"))
            v.wait_ge(*step("nlam"))
            def softmax(u):
                s = SC[u % 2]
                s3 = three(s, T)
                z = bank(u % 2)
                v.wait_ge(S("scores"), u + 1)
                if u >= 10:
                    v.wait_ge(S("pa"), u - 5)
                elif u >= 3:
                    v.wait_ge(S("pa"), (u - 1) // 2)
                if u < 8:
                    slope = 2.0 ** (-8.0 * (u // 2 + 1) / NH)
                    stt(s, const("dist"), -slope, z, ALU.mult, ALU.add).then_inc(S("sc_in"), 1)
                else:
                    v.wait_ge(S("window"), 1)
                    tt(s, NB[:, 512 * (u - 8):512 * (u - 8) + 512], z, ALU.add).then_inc(S("sc_in"), 1)
                v.wait_ge(S("sc_in"), u + 1)
                v.tensor_reduce(nmx[:, 2 * (u % 2):2 * (u % 2) + 2], s3, AX_X, ALU.max, negate=True).then_inc(S("nmax"), 1)

            def weigh(u):
                v.wait_ge(S("probs"), 2 * u + 2)
                r = rcs[:, 2 * (u % 2):2 * (u % 2) + 2]
                link(v.reciprocal(r, sme[:, 2 * (u % 2):2 * (u % 2) + 2]))
                s3 = three(SC[u % 2], T)
                w = u // 2 if u < 8 else u - 4
                pa3 = three(PA[w % 2], T)
                if w >= 2:
                    v.wait_ge(S("pat"), w - 1)
                if u < 8 and u % 2:
                    link(ts(r, r, nlam, None, ALU.mult))
                    for t in range(T):
                        last = stt(pa3[:, t, :], s3[:, t, :], r[:, t:t + 1], pa3[:, t, :], ALU.mult, ALU.add)
                    last.then_inc(S("pa"), 1)
                    v.wait_ge(S("pa"), w + 1)
                elif u < 8:
                    for t in range(T):
                        link(ts(pa3[:, t, :], s3[:, t, :], r[:, t:t + 1], None, ALU.mult))
                else:
                    for t in range(T):
                        last = ts(pa3[:, t, :], s3[:, t, :], r[:, t:t + 1], None, ALU.mult)
                    last.then_inc(S("pa"), 1)

            softmax(0)
            for u in range(1, 16):
                softmax(u)
                weigh(u - 1)
            weigh(15)
            v.wait_ge(*step("dsum"))
            link(ts(DRS, bank(0, 2), 1.0 / P, EPS, ALU.mult, ALU.add))
            v.reciprocal(DRS, DRS).then_inc(*signal("drinv"))
            v.wait_ge(*step("do"))
            link(ts(DO, DO, vec("subln"), 1.0 - 0.2, ALU.mult, ALU.mult))
            v.wait_ge(*step("drstd"))
            tt(YT[:, 0:4, :], three(DO, NH), three(DRS, NH), ALU.mult).then_inc(*signal("y_diff"))

            def gated(which, ready, gate, signal):
                v.wait_ge(S("ssq"), SQUARES[which])
                s4 = ssq.rearrange("p (t h) -> p t h", t=T)
                link(tt(mean.unsqueeze(2), s4[:, :, 0:1], s4[:, :, 1:2], ALU.add))
                link(ts(mean, mean, 1.0 / D, EPS, ALU.mult, ALU.add))
                v.reciprocal(mean, mean).then_inc(S("rinv"), 1)
                v.wait_ge(S("rstd"), NORMS.index(which) + 1)
                for t in range(T):
                    for h in range(2):
                        hs = slice(512 * h, 512 * h + 512)
                        link(stt(XN[:, t, hs], bank(2 * t + h), rstd[:, t:t + 1], gate[:, hs], ALU.mult, ALU.mult))
                    tt(X[:, t, :], X[:, t, :], XN[:, t, :], ALU.add).then_inc(S(signal), 1)

            gated("m", None, G1B, "x4")
            v.wait_ge(S("x4"), T)
            dve_norm(link, 4, GW2, MODC[:, 16:24])
            v.wait_ge(S("b1_parts"), 7)
            v.memset(IR[:, :, 4:8], -3.0e38)
            link(v.memset(LX[:, :, 32:36], -3.0e38))
            v.wait_ge(*step("lg"))
            link(tt(LG, three(flat[:, 2048:2112], T), vec("brt").unsqueeze(1).broadcast_to([P, T, NE]), ALU.add))
            link(v.tensor_copy(LX[:, :, 0:32], LG))
            for t in range(T):
                link(v.max(V8[:, t, :], LG[:, t, :]))
            link(v.tensor_copy(IR[:, :, 0:4], V8[:, :, 0:4]))
            for t in range(T):
                link(v.match_replace(MR[:, t, 0:36], IR[:, t, :], LX[:, t, 0:36], 3.0e38))
            tt(MASK, MR[:, :, 0:32], LG, ALU.not_equal).then_inc(*signal("mask"))
            tt(EE, LG, V8[:, :, 0:1].broadcast_to([P, T, NE]), ALU.subtract).then_inc(*signal("lgs"))
            v.wait_ge(*step("mask"))
            v.wait_ge(*step("ee"))
            link(tt(EE, EE, MASK, ALU.mult))
            link(v.tensor_reduce(GSUM, EE, AX_X, ALU.add))
            link(v.reciprocal(GSUM, GSUM))
            tt(GATE, EE, GSUM.unsqueeze(2).broadcast_to([P, T, NE]), ALU.mult).then_inc(S("gate"), 1)
            v.wait_ge(*step("pos"))
            link(stt(PM, MASK, -1000.0, three(flat[:, 2560:2624], T), ALU.mult, ALU.add))
            ts(PM, PM, 1000.0, None, ALU.add).then_inc(S("gate"), 1)
            cnt = flat[0:32, 2624:2625]
            link(ts(CNR[0:32], cnt, float(CAP), 1.0, ALU.is_gt, ALU.add))
            for i in range(2, L // CAP):
                link(stt(CNR[0:32], cnt, float(CAP * i), CNR[0:32], ALU.is_gt, ALU.add))
            ts(CNR[0:32], CNR[0:32], 0.0, None, ALU.add).then_inc(*signal("cnr"))
            v.wait_ge(*step("cum"))
            v.wait_ge(*step("cnr"))
            link(v.tensor_copy(CCE[0:32], flat[0:32, 3072:3073]))
            v.tensor_copy(passes[0:1, 0:32], flat[0:1, 3073:3105])
            ts(passes[0:1, 32:64], flat[0:1, 3105:3137], -1.0, None, ALU.add)
            v.tensor_copy(passes[0:1, 64:65], flat[0:1, 3137:3138]).then_inc(*signal("cum_in"))
            link(tt(CCI[0:32], CCE[0:32], CNR[0:32], ALU.add))
            count = const("count")[0:32, :]
            link(ts(OH[0:32], count, CCI[0:32], None, ALU.is_lt))
            stt(OH[0:32], count, CCE[0:32], OH[0:32], ALU.is_ge, ALU.mult).then_inc(S("oh"), 1)
            link(ts(RM[0:32], count, CCE[0:32], -float(CAP), ALU.subtract, ALU.mult))
            v.wait_ge(S("oh"), 1)
            tt(RM[0:32], RM[0:32], OH[0:32], ALU.mult).then_inc(S("oh"), 1)
            for part in (1, 2):
                link(v.tensor_copy(OH[NE * part:NE * part + NE, :], OH[0:NE, :]))
            v.wait_ge(*step("pmt"))
            link(v.tensor_copy(PMT[0:32], flat[0:32, 3584:3840]))
            v.tensor_copy(GTT[0:32], flat[0:32, 3840:4096]).then_inc(S("pmt_in"), 1)
            v.wait_ge(S("h2r"), 1)
            v.tensor_copy(H2R[:, 0, :], bank(0, 2)).then_inc(S("h2r_in"), 1)
            v.wait_ge(*step("pp"))
            link(v.tensor_copy(PP, three(flat[:, 2048:2048 + T * NPMAX], T)))
            link(v.tensor_copy(GP, three(flat[:, 2176:2176 + T * NPMAX], T)))
            v.memset(SGT, 0.0).then_inc(S("sgt_in"), 1)
            v.memset(YS, 0.0).then_inc(S("y_in"), 1)
            slot = const("slot")

            def select(p):
                for t in range(T):
                    last = ts(SEL[:, t, :], slot[:, 0:CAP], PP[:, t, bass.ds(p, 1)], None, ALU.is_equal)
                last.then_inc(S("sel"), 1)

            def select_gated(p):
                v.tensor_copy(OHB[0:3 * NE, :], OH[0:3 * NE, bass.ds(p, 1)].broadcast_to([3 * NE, CAP])).then_inc(S("ohb"), 1)
                for t in range(T):
                    last = ts(SG[:, t, :], slot, PP[:, t, bass.ds(p, 1)], GP[:, t, bass.ds(p, 1)], ALU.is_equal, ALU.mult)
                last.then_inc(S("sg"), 1)

            def swiglu(p):
                v.wait_ge(S("w1"), p + 1)
                ts(GLU, flat[:, 2048:2304], 7.0, None, ALU.min).then_inc(S("glu"), 1)
                ts(LIN, flat[:, 2304:2560], 7.0, -7.0, ALU.min, ALU.max).then_inc(S("lin"), 1)
                v.wait_ge(S("lin"), p + 1)
                v.wait_ge(S("glu"), p + 1)
                stt(HID, LIN, 1.0, GLU, ALU.add, ALU.mult).then_inc(S("hid"), 1)
                v.wait_ge(S("hid"), p + 1)
                v.wait_ge(S("sig"), p + 1)
                tt(HID, HID, SIG, ALU.mult).then_inc(S("act"), 1)

            select(0)
            select_gated(0)
            v.wait_ge(S("g"), 1)
            v.tensor_copy(GS, flat[:, 3072:3328]).then_inc(S("g_in"), 1)
            v.wait_ge(*step("cum_in"))
            n_passes = v.value_load(passes[0:1, 64:65], min_val=NE, max_val=NPMAX - 1)
            with v.Fori(0, n_passes) as p:
                v.wait_ge(S("g"), p + 1)
                select(p + 1)
                swiglu(p)
                v.wait_ge(S("g"), p + 2)
                v.wait_ge(S("h"), p + 1)
                v.tensor_copy(GS, flat[:, 3072:3328]).then_inc(S("g_in"), 1)
                v.wait_ge(S("sgtp"), p + 1)
                select_gated(p + 1)
            gated("e", None, G2B, "x5")



def _constants():
    c = np.zeros((P, NCONST), np.float32)
    i, j = np.arange(P)[:, None], np.arange(P)[None, :]

    def put(name, a):
        o, w = CO[name]
        c[:, o:o + w] = a

    chunk = (i // GCH) == (j // GCH)
    put("ident", i == j)
    put("ones", 1.0)
    put("before", i < j)
    put("after", i > j)
    put("slot", j % CAP)
    put("row", np.broadcast_to(i, (P, 64)))
    put("count", np.broadcast_to(np.arange(NPMAX)[None], (P, NPMAX)))
    put("upto", (i <= j) & chunk)
    put("same", chunk)
    lv = []
    for l in range(6):
        s = 1 << l
        lv.append(-1.0 * (((i // (2 * s)) == (j // (2 * s))) & ((i // s) % 2 == 0) & ((j // s) % 2 == 1)))
    put("level", np.concatenate(lv, 1))
    put("dist", np.concatenate([np.abs(np.arange(L)[None] - (P * t + i)) for t in range(T)], 1))
    col = np.arange(P)[:, None] % 64
    start = np.clip(col - 8, 0, 48)
    cc = np.arange(64)[None]
    put("window", np.where((cc >= start) & (cc < start + 16), 0.0, -BIG))
    return c


def _layout(inputs):
    g = {k: np.asarray(v) for k, v in inputs.items()}

    def cols(v):
        return v.reshape(-1, P).T

    vec = np.zeros((P, NVEC), np.float32)

    def put(name, a):
        o, w = VO[name]
        vec[:a.shape[0], o:o + w] = a

    put("norm_mix", cols(g["w_norm_mix"][0]))
    put("norm_ffn", cols(g["w_norm_ffn"][0]))
    put("pre_mix", cols(g["g_pre_mix_2"][0]))
    put("pre_ffn", cols(g["g_pre_ffn_2"][0]))
    put("sconv", g["w_sconv"][0].reshape(3, 2, P).transpose(2, 1, 0).reshape(P, 6))
    gc = g["w_gdn_conv"][0].reshape(4, 3, 4, P)[:, [1, 0, 2]]
    put("gconv", gc.transpose(3, 1, 2, 0).reshape(P, 48))
    put("gnorm", g["w_gdn_norm"][0][:, None])
    put("subln", g["g_subln_2"][0][:, None])
    put("lam", np.stack([g[n][0] for n in ("lam_q1_2", "lam_q2_2", "lam_k1_2", "lam_k2_2")], 1))
    put("c", cols(g["c_2"][0]))
    win = g["w_mix_in"][0]
    put("ab", win[:, 2816:2824].reshape(KC, P, 8).transpose(1, 0, 2).reshape(P, 64))
    put("alog", np.broadcast_to(g["gdn_a_log"], (P, 4)))
    put("dtb", np.broadcast_to(g["gdn_dt_bias"], (P, 4)))
    put("brt", np.broadcast_to(g["b_router_2"], (P, NE)))
    fc = g["w_ffn_conv"][0].reshape(3, 2, PUP, 2, P)
    put("fconv", fc.transpose(4, 2, 1, 3, 0).reshape(P, PUP * 12))
    put("router", g["w_router_2"][0].reshape(KC, P, NE).transpose(1, 0, 2).reshape(P, KC * NE))

    def by_columns(w):
        return w.reshape(KC, P, -1, 512).transpose(2, 1, 0, 3).reshape(-1, P, NPIECE)

    def by_rows(w):
        return w.reshape(-1, 4, P, 1024).transpose(0, 2, 1, 3).reshape(-1, P, NPIECE)

    def sl(a, n):
        return win[:, a:a + n]

    order = np.concatenate([sl(768 + 512, 512), sl(768, 512), sl(768 + 1024, 512), sl(768 + 1536, 512),
                            sl(256, 512), sl(0, 256), sl(2824, 256), sl(2824 + 256, 512)], 1)
    up = g["w_ffn_up"][0].reshape(D, 2, PUP, 256).transpose(0, 2, 1, 3).reshape(D, 2 * DFF)
    down = np.concatenate([g["w_ffn_down"][0], np.zeros((256, D), np.float32)])
    w_in2 = g["w_in_2"][0]
    two = np.concatenate([w_in2[:, 0:1024], w_in2[:, 1536:2560], w_in2[:, 1024:1536], w_in2[:, 2560:3072]], 1)
    stream = np.concatenate([by_columns(order), by_columns(g["w_ada_2"][0]), by_rows(g["w_mix_out"][0]),
                             by_columns(up), by_rows(down), by_columns(two), by_rows(g["w_out_2"][0])])
    assert stream.shape[0] == NSTREAM
    bada = np.broadcast_to(g["b_ada_2"][0].reshape(3, 4, 1, 512).transpose(1, 2, 0, 3), (4, 32, 3, 512))
    rows = np.stack([g["w_norm_final"], g["g_post_mix_2"][0], g["g_post_ffn_2"][0]]).reshape(1, 3072)
    r, c = np.arange(4), np.arange(64)
    dr = (r[None, :] - r[:, None]) + 7
    dc = np.clip(c[None, :] - c[:, None], -15, 15) + 15
    nb = g["nat_rpb_2"][0][:, dr[:, None, :, None], dc[None, :, None, :]].reshape(8, T, P, L)
    w1 = g["w1_2"][0].reshape(NE, 4, 2, P, 4, 256, 2).transpose(0, 1, 3, 2, 4, 6, 5).reshape(NE * 4, P, NPIECE)
    w2 = g["w2_2"][0].reshape(NE, 2, 4, P, 1024).transpose(0, 1, 3, 2, 4).reshape(NE * 2, P, NPIECE)
    b1 = g["b1_2"][0].reshape(NE, 4, 256, 2).transpose(0, 1, 3, 2).reshape(NE, 2048)
    return {
        "consts": _constants(), "vecs": vec, "stream": stream, "bada": bada.reshape(P, 1536),
        "rows": np.broadcast_to(rows, (P, 3072)), "natb": nb.transpose(2, 0, 1, 3).reshape(P, 4096),
        "w1": w1, "w2": w2, "b1": b1, "b2": g["b2_2"][0],
        "x": g["x"][0].reshape(T, P, D).transpose(1, 0, 2).reshape(P, T * D),
    }


def kernel(**inputs):
    import concourse.bacc as bacc
    from concourse.bass_utils import run_bass_kernel_spmd

    nc = bacc.Bacc("TRN2", target_bir_lowering=False, num_devices=1)
    arrays, args = {}, {}
    for name, a in _layout(inputs).items():
        arrays["in_" + name] = np.ascontiguousarray(a)
        args[name] = nc.dram_tensor("in_" + name, a.shape, mybir.dt.from_np(a.dtype), kind="ExternalInput").ap()
    args["out"] = nc.dram_tensor("out_0", (P, T * D), F32, kind="ExternalOutput").ap()
    first_block_and_moe(nc, **args)
    got = run_bass_kernel_spmd(nc, [arrays], core_ids=[0]).results[0]["out_0"]
    return got.reshape(P, T, D).transpose(1, 0, 2).reshape(1, L, D)
```
